# Optimizing a Trainium2 kernel written in Bass

```python
import math
import jax, jax.numpy as jnp
from jax import lax
import numpy as np

D_MODEL = 1024
BATCH = 1
SEQ = 512
DEPTH = 2

N_MIXERS = 2
N_RET_LAYERS = (DEPTH + 1) // 2
N_DIFF_LAYERS = DEPTH // 2
RMS_EPS = 1e-6

RET_HEADS = 4
RET_DK = D_MODEL // RET_HEADS
RET_DV = 2 * RET_DK
RET_CHUNK = 128
ROPE_BASE = 10000.0
RET_IN = 2 * RET_HEADS * RET_DK + 2 * RET_HEADS * RET_DV

DIFF_HEADS = 8
DIFF_DH = D_MODEL // (2 * DIFF_HEADS)
DIFF_DV = 2 * DIFF_DH
DIFF_IN = 4 * DIFF_HEADS * DIFF_DH + DIFF_HEADS * DIFF_DV
Q_BLOCK = 128
NEG_BIG = -1e30

REL_BUCKETS = 32
REL_MAX_EXACT = REL_BUCKETS // 2
REL_MAX_DIST = 128

D_FF = -(-8 * D_MODEL // (3 * 256)) * 256

kernel_name = "hybrid_retention_diffattn_sandwich"

def rmsnorm(x, g):
    xf = x.astype(jnp.float32)
    y = xf * lax.rsqrt(jnp.mean(xf * xf, axis=-1, keepdims=True) + RMS_EPS)
    return (y * g.astype(jnp.float32)).astype(x.dtype)

def rms_unit(xf):
    return xf * lax.rsqrt(jnp.mean(xf * xf, axis=-1, keepdims=True) + RMS_EPS)

def rotary(x, pos):
    half = x.shape[-1] // 2
    inv = ROPE_BASE ** (-jnp.arange(half, dtype=jnp.float32) / half)
    ang = pos[:, None] * inv[None, :]
    cos, sin = jnp.cos(ang), jnp.sin(ang)
    x1, x2 = x[..., :half], x[..., half:]
    return jnp.concatenate([x1 * cos - x2 * sin, x1 * sin + x2 * cos], axis=-1)

def retention_mixer(h, w_in, w_out):
    B, S, _ = h.shape
    H, C = RET_HEADS, RET_CHUNK
    n_chunks = S // C
    proj = h @ w_in
    q, k, v, gate = jnp.split(
        proj, [H * RET_DK, 2 * H * RET_DK, 2 * H * RET_DK + H * RET_DV], axis=-1)
    pos = jnp.arange(S, dtype=jnp.float32)
    q = q.astype(jnp.float32).reshape(B, S, H, RET_DK).transpose(0, 2, 1, 3)
    k = k.astype(jnp.float32).reshape(B, S, H, RET_DK).transpose(0, 2, 1, 3)
    v = v.astype(jnp.float32).reshape(B, S, H, RET_DV).transpose(0, 2, 1, 3)
    q = rotary(q, pos)
    k = rotary(k, pos) * (RET_DK ** -0.5)

    log_gamma = jnp.log1p(-(2.0 ** (-5.0 - jnp.arange(H, dtype=jnp.float32))))
    idx = jnp.arange(C, dtype=jnp.float32)
    diff = idx[:, None] - idx[None, :]
    decay_mask = jnp.where(diff[None] >= 0,
                           jnp.exp(jnp.maximum(diff, 0.0)[None] * log_gamma[:, None, None]),
                           0.0)
    q_decay = jnp.exp((idx[None, :] + 1.0) * log_gamma[:, None])[None, :, :, None]
    k_decay = jnp.exp((C - 1.0 - idx[None, :]) * log_gamma[:, None])[None, :, :, None]
    chunk_decay = jnp.exp(C * log_gamma)[None, :, None, None]

    def to_chunks(t):
        return t.reshape(B, H, n_chunks, C, t.shape[-1]).transpose(2, 0, 1, 3, 4)

    def step(state, inp):
        qc, kc, vc = inp
        inner = jnp.einsum('bhnd,bhmd->bhnm', qc, kc) * decay_mask[None]
        out = jnp.einsum('bhnm,bhme->bhne', inner, vc)
        out = out + jnp.einsum('bhnd,bhde->bhne', qc, state) * q_decay
        state = state * chunk_decay + jnp.einsum('bhmd,bhme->bhde', kc * k_decay, vc)
        return state, out

    state0 = jnp.zeros((B, H, RET_DK, RET_DV), jnp.float32)
    _, ys = lax.scan(step, state0, (to_chunks(q), to_chunks(k), to_chunks(v)))
    y = ys.transpose(1, 0, 3, 2, 4).reshape(B, S, H, RET_DV)
    y = rms_unit(y).reshape(B, S, H * RET_DV)
    y = y * jax.nn.silu(gate.astype(jnp.float32))
    return y.astype(h.dtype) @ w_out

def t5_causal_bucket(rel):
    n = jnp.maximum(rel, 0)
    nf = jnp.maximum(n, 1).astype(jnp.float32)
    large = REL_MAX_EXACT + (jnp.log(nf / REL_MAX_EXACT)
                             / math.log(REL_MAX_DIST / REL_MAX_EXACT)
                             * (REL_BUCKETS - REL_MAX_EXACT)).astype(jnp.int32)
    large = jnp.minimum(large, REL_BUCKETS - 1)
    return jnp.where(n < REL_MAX_EXACT, n, large)

def diff_attention_mixer(h, w_in, w_out, lam, subln_g, rel_table, lambda_init):
    B, S, _ = h.shape
    H, d = DIFF_HEADS, DIFF_DH
    nb = S // Q_BLOCK
    proj = h @ w_in
    q, k, v = jnp.split(proj, [2 * H * d, 4 * H * d], axis=-1)
    q = q.reshape(B, S, H, 2, d).transpose(0, 2, 3, 1, 4) * (d ** -0.5)
    k = k.reshape(B, S, H, 2, d).transpose(0, 2, 3, 1, 4)
    v = v.reshape(B, S, H, DIFF_DV).transpose(0, 2, 1, 3)
    lamf = lam.astype(jnp.float32)
    lam_full = (jnp.exp(jnp.sum(lamf[0] * lamf[1])) - jnp.exp(jnp.sum(lamf[2] * lamf[3]))
                + lambda_init)
    q_blocks = q.reshape(B, H, 2, nb, Q_BLOCK, d).transpose(3, 0, 1, 2, 4, 5)
    k_pos = jnp.arange(S, dtype=jnp.int32)

    def block(args):
        qb, bi = args
        q_pos = bi * Q_BLOCK + jnp.arange(Q_BLOCK, dtype=jnp.int32)
        rel = q_pos[:, None] - k_pos[None, :]
        bias = rel_table[t5_causal_bucket(rel)].astype(jnp.float32).transpose(2, 0, 1)
        logits = jnp.einsum('bhiqd,bhikd->bhiqk', qb, k).astype(jnp.float32)
        logits = logits + bias[None, :, None]
        logits = jnp.where(rel[None, None, None] >= 0, logits, NEG_BIG)
        p = jax.nn.softmax(logits, axis=-1)
        attn = p[:, :, 0] - lam_full * p[:, :, 1]
        return jnp.einsum('bhqk,bhkd->bhqd', attn.astype(v.dtype), v)

    o = lax.map(block, (q_blocks, jnp.arange(nb, dtype=jnp.int32)))
    o = o.transpose(1, 2, 0, 3, 4).reshape(B, H, S, DIFF_DV)
    o = rmsnorm(o, subln_g) * (1.0 - lambda_init)
    o = o.transpose(0, 2, 1, 3).reshape(B, S, H * DIFF_DV)
    return o @ w_out

def swiglu(h, w_gate, w_up, w_down):
    return (jax.nn.silu(h @ w_gate) * (h @ w_up)) @ w_down

def setup_inputs(seed: int = 0) -> dict:
    key = jax.random.key(seed)
    ks = jax.random.split(key, 12)
    f32 = jnp.float32
    nrm = jax.random.normal
    return {
        "x": nrm(ks[0], (BATCH, SEQ, D_MODEL), f32),
        "norm_gains": 1.0 + 0.05 * nrm(ks[1], (DEPTH, 4, D_MODEL), f32),
        "ret_w_in": nrm(ks[2], (N_RET_LAYERS, D_MODEL, RET_IN), f32) * D_MODEL ** -0.5,
        "ret_w_out": nrm(ks[3], (N_RET_LAYERS, RET_HEADS * RET_DV, D_MODEL), f32)
                     * (RET_HEADS * RET_DV) ** -0.5,
        "diff_w_in": nrm(ks[4], (N_DIFF_LAYERS, D_MODEL, DIFF_IN), f32) * D_MODEL ** -0.5,
        "diff_w_out": nrm(ks[5], (N_DIFF_LAYERS, DIFF_HEADS * DIFF_DV, D_MODEL), f32)
                      * (DIFF_HEADS * DIFF_DV) ** -0.5,
        "diff_lambda": 0.1 * nrm(ks[6], (N_DIFF_LAYERS, 4, DIFF_DH), f32),
        "diff_subln": 1.0 + 0.05 * nrm(ks[7], (N_DIFF_LAYERS, DIFF_DV), f32),
        "rel_bias_table": 0.5 * nrm(ks[8], (REL_BUCKETS, DIFF_HEADS), f32),
        "ffn_w_gate": nrm(ks[9], (DEPTH, D_MODEL, D_FF), f32) * D_MODEL ** -0.5,
        "ffn_w_up": nrm(ks[10], (DEPTH, D_MODEL, D_FF), f32) * D_MODEL ** -0.5,
        "ffn_w_down": nrm(ks[11], (DEPTH, D_FF, D_MODEL), f32) * D_FF ** -0.5,
    }

def reference(x, norm_gains, ret_w_in, ret_w_out, diff_w_in, diff_w_out, diff_lambda,
              diff_subln, rel_bias_table, ffn_w_gate, ffn_w_up, ffn_w_down):
    for i in range(DEPTH):
        g = norm_gains[i]
        h = rmsnorm(x, g[0])
        j = i // N_MIXERS
        if i % N_MIXERS == 0:
            m = retention_mixer(h, ret_w_in[j], ret_w_out[j])
        else:
            lambda_init = 0.8 - 0.6 * math.exp(-0.3 * i)
            m = diff_attention_mixer(h, diff_w_in[j], diff_w_out[j], diff_lambda[j],
                                     diff_subln[j], rel_bias_table, lambda_init)
        x = x + rmsnorm(m, g[1])
        h = rmsnorm(x, g[2])
        x = x + rmsnorm(swiglu(h, ffn_w_gate[i], ffn_w_up[i], ffn_w_down[i]), g[3])
    return x


_drawn_inputs = setup_inputs


def setup_inputs(seed=0):
    import zlib

    import numpy as np

    out = dict(_drawn_inputs(seed))
    spreads = {}
    factors = {}
    for name, (base, spread) in spreads.items():
        noise = np.random.default_rng([zlib.crc32(name.encode()), seed]).standard_normal(out[name].shape)
        drawn = base * np.exp(spread * noise) if base else spread * noise
        out[name] = __import__('jax').numpy.asarray(drawn.astype(out[name].dtype))
    for name, factor in factors.items():
        out[name] = (out[name] * factor).astype(out[name].dtype)
    return out
```

```python
from contextlib import ExitStack

import concourse.bass as bass
import numpy as np
from concourse import mybir

F32 = mybir.dt.float32
F32R = mybir.dt.float32r
BF16 = mybir.dt.bfloat16
ACT = mybir.ActivationFunctionType
ALU = mybir.AluOpType
AX_X = mybir.AxisListType.X

P = 128
S = 512
D = 1024
ST = S // P
KT = D // P
EPS = 1e-6
BANK = 512

RET_HEADS = 4
RET_DK = D // RET_HEADS
RET_DV = 2 * RET_DK

DIFF_HEADS = 8
DIFF_DH = D // (2 * DIFF_HEADS)
DIFF_DV = 2 * DIFF_DH
GROUP = 2
GROUPS = DIFF_HEADS // GROUP
LAMBDA_INIT = 0.8 - 0.6 * float(np.exp(-0.3))
BUCKETS = 32
MASKED = 1e30

D_FF = -(-8 * D // (3 * 256)) * 256
FT = D_FF // P

UNIT = 2048
PACKED = S + 384 + P + 256
OFF = {3: 0, 2: 512, 0: 896, 1: 1024}

RET_U = 0
RET_N = 6
RETO_U = RET_U + RET_N * RET_HEADS
RETO_N = RET_HEADS * RET_DV // (2 * P)
FFN_N = FT // 2
GU_U = [RETO_U + RETO_N, 0]
DN_U = [GU_U[0] + 2 * FFN_N, 0]
DIFF_U = DN_U[0] + FFN_N
DIFF_N = 4
DIFFO_U = DIFF_U + DIFF_N * GROUPS
DIFFO_N = KT // 2
GU_U[1] = DIFFO_U + DIFFO_N
DN_U[1] = GU_U[1] + 2 * FFN_N
UNITS = DN_U[1] + FFN_N
CLOSERS = [(RETO_U, RETO_N), (DN_U[0], FFN_N), (DIFFO_U, DIFFO_N), (DN_U[1], FFN_N)]
CLOSER_BASE = [sum(n for _, n in CLOSERS[:c]) for c in range(4)]

PRIME = 2


def unit_size(u):
    return UNIT // 2 if DIFF_U <= u < DIFFO_U and (u - DIFF_U) % DIFF_N >= 2 else UNIT


def build(nc, A, out):
    bias_rows = nc.dram_tensor("bias_rows", (DIFF_HEADS, 640), F32, kind="Internal").ap()
    bias_tiles = nc.dram_tensor("bias_tiles", (DIFF_HEADS, P, S), F32, kind="Internal").ap()

    with ExitStack() as ctx:
        def sb(name, shape, dt=F32, within=ctx):
            return within.enter_context(nc.sbuf_tensor(name, shape, dt))

        def sem(name):
            return ctx.enter_context(nc.semaphore(name))

        x = sb("x", [P, ST, D])
        h_hi = sb("h_hi", [P, KT, S], F32R)
        h_lo = sb("h_lo", [P, KT, S], F32R)
        raw = [sb(f"raw{i}", [P, UNIT]) for i in range(2)]
        w_hi = [sb(f"w_hi{i}", [P, UNIT], F32R) for i in range(2)]
        w_lo = [sb(f"w_lo{i}", [P, UNIT], F32R) for i in range(2)]
        g_pre = sb("g_pre", [P, D])
        tmp = sb("tmp", [P, 3, D])
        ident = sb("ident", [P, P])
        junk = sb("junk", [P, D], BF16)
        ssq = sb("ssq", [P, 16])
        rstd = sb("rstd", [P, 16])
        expo = sb("expo", [P, ST])
        eps = sb("eps", [P, ST])
        lam = sb("lam", [P, 8])
        subg = sb("subg", [P, 2])
        rel = sb("rel", [BUCKETS + 1, DIFF_HEADS])
        stat = sb("stat", [P, 32])
        with ExitStack() as one:
            cs = sb("cs", [P, 2, S], within=one)
        g_post = sb("g_post", [P, D])
        with ExitStack() as ret:
            qk_hi = sb("qk_hi", [P, 4, S], F32R, ret)
            qk_lo = sb("qk_lo", [P, 4, S], F32R, ret)
            rv_hi = sb("rv_hi", [P, ST, RET_DV], F32R, ret)
            rv_lo = sb("rv_lo", [P, ST, RET_DV], F32R, ret)
            in_hi = sb("in_hi", [P, PACKED], F32R, ret)
            in_lo = sb("in_lo", [P, PACKED], F32R, ret)
            decay = sb("decay", [P, PACKED], within=ret)
            gated = sb("gated", [P, ST, RET_DV], within=ret)
            yT = sb("yT", [P, RET_HEADS * RET_DV // P, S], within=ret)
        with ExitStack() as diff:
            q_hi = sb("q_hi", [P, GROUP, S], F32R, diff)
            q_lo = sb("q_lo", [P, GROUP, S], F32R, diff)
            k_hi = sb("k_hi", [P, GROUP, S], F32R, diff)
            k_lo = sb("k_lo", [P, GROUP, S], F32R, diff)
            v_hi = sb("v_hi", [P, ST, GROUP * DIFF_DV], F32R, diff)
            v_lo = sb("v_lo", [P, ST, GROUP * DIFF_DV], F32R, diff)
            aT_hi = sb("aT_hi", [P, PACKED], F32R, diff)
            aT_lo = sb("aT_lo", [P, PACKED], F32R, diff)
            nbias = [sb(f"nbias{j}", [P, S], within=diff) for j in range(GROUP)]
            lg = sb("lg", [P, 2, PACKED], within=diff)
            o_n = [sb(f"o_n{j}", [P, ST, P], within=diff) for j in range(GROUP)]
            oT = sb("oT", [P, KT, S], within=diff)
        with ExitStack() as ffn:
            hidden = sb("hidden", [P, FT, S], within=ffn)
            sil = sb("sil", [P, 2, S], within=ffn)

        ps = ctx.enter_context(nc.psum_tensor("ps", [P, 8 * BANK], F32))

        def bank(b, n=1):
            return ps[:, b * BANK:(b + n) * BANK]

        def scores(t, i):
            at = 4 * BANK + 256 * i if t == 1 else 2 * BANK * i + OFF[t]
            return ps[:, at:at + (t + 1) * P]

        raw_in = [sem(f"raw_in{i}") for i in range(2)]
        w_hi_made = sem("w_hi_made")
        w_split = sem("w_split")
        w_used = sem("w_used")
        a_hi_made = sem("a_hi_made")
        a_split = sem("a_split")
        x_in = [sem(f"x_in{t}") for t in range(ST)]
        const_in = sem("const_in")
        cs_in = sem("cs_in")
        gpre_in = sem("gpre_in")
        gpost_in = sem("gpost_in")
        rel_in = sem("rel_in")
        lam_in = sem("lam_in")
        decay_in = sem("decay_in")
        nbias_in = [sem(f"nbias_in{j}") for j in range(GROUP)]
        bias_stored = sem("bias_stored")
        bias_spread = sem("bias_spread")
        out_done = sem("out_done")
        set_up = sem("set_up")
        bias_mm = sem("bias_mm")
        bias_cp = sem("bias_cp")
        lam_sum = sem("lam_sum")
        lam_exp = sem("lam_exp")
        lam_made = sem("lam_made")
        row_done = sem("row_done")
        post_ssq = sem("post_ssq")
        post_ms = sem("post_ms")
        post_rstd = sem("post_rstd")
        post_scaled = sem("post_scaled")
        x_added = sem("x_added")
        pre_ssq = sem("pre_ssq")
        pre_ms = sem("pre_ms")
        pre_rstd = sem("pre_rstd")
        pre_scaled = sem("pre_scaled")
        pre_turned = sem("pre_turned")
        h_hi_made = sem("h_hi_made")
        h_split = sem("h_split")
        rot_mul = sem("rot_mul")
        rot_made = sem("rot_made")
        qk_hi_made = sem("qk_hi_made")
        qk_split = sem("qk_split")
        inner_mm = sem("inner_mm")
        inner_made = sem("inner_made")
        inner_hi_made = sem("inner_hi_made")
        inner_split = sem("inner_split")
        rv_row = sem("rv_row")
        rv_hi_made = sem("rv_hi_made")
        rv_split = sem("rv_split")
        ret_mm = sem("ret_mm")
        ret_ssq = sem("ret_ssq")
        ret_ms = sem("ret_ms")
        ret_rstd = sem("ret_rstd")
        gate_row = sem("gate_row")
        gate_made = sem("gate_made")
        y_made = sem("y_made")
        y_turned = sem("y_turned")
        yT_made = sem("yT_made")
        q_hi_made = sem("q_hi_made")
        q_split = sem("q_split")
        k_hi_made = sem("k_hi_made")
        k_split = sem("k_split")
        v_hi_made = sem("v_hi_made")
        v_split = sem("v_split")
        qk_mm = sem("qk_mm")
        shared_bank = sem("shared_bank")
        lg_made = sem("lg_made")
        exp_made = sem("exp_made")
        recip_made = sem("recip_made")
        lam_scaled = sem("lam_scaled")
        e1_scaled = sem("e1_scaled")
        attn_made = sem("attn_made")
        a_turned = sem("a_turned")
        aT_hi_made = sem("aT_hi_made")
        aT_split = sem("aT_split")
        o_mm = sem("o_mm")
        o_sq = sem("o_sq")
        o_ssq = sem("o_ssq")
        o_ms = sem("o_ms")
        o_rstd = sem("o_rstd")
        o_normed = sem("o_normed")
        o_turned = sem("o_turned")
        oT_made = sem("oT_made")
        sil_made = sem("sil_made")
        hid_made = sem("hid_made")

        ret_in_w = A["ret_w_in"][0].rearrange("(k p) n -> p k n", p=P)
        diff_in_w = A["diff_w_in"][0].rearrange("(k p) n -> p k n", p=P)
        gate_w = [A["ffn_w_gate"][l].rearrange("(k p) n -> p k n", p=P) for l in range(2)]
        up_w = [A["ffn_w_up"][l].rearrange("(k p) n -> p k n", p=P) for l in range(2)]
        close_w = [w.rearrange("(k p) n -> p k n", p=P) for w in (
            A["ret_w_out"][0], A["ffn_w_down"][0], A["diff_w_out"][0], A["ffn_w_down"][1])]

        def spread(src, n):
            return bass.AP(tensor=src.tensor, offset=src.offset, ap=[[0, P], [1, n]])

        def closing_steps(c, step, eng):
            n = CLOSERS[c][1]
            pairs = (n - 2) // 2
            step(0, 0)
            with eng.Fori(0, pairs) as i:
                for j in (1, 2):
                    step(2 * i + j, j)
            for u in range(1 + 2 * pairs, n):
                step(u, u)

        block = ctx.enter_context(nc.Block())

        @block.sync
        def _(sp):
            def load(u, slot, src, free=True):
                if free:
                    sp.wait_ge(w_split, u - 1 + PRIME)
                k, n = src.shape[1], src.shape[2]
                dst = raw[slot][:, 0:k * n].rearrange("p (k n) -> p k n", k=k)
                sp.dma_start(dst, src).then_inc(raw_in[slot], 16)

            with sp.Fori(0, RET_HEADS) as h:
                u = RET_U + RET_N * h
                load(u, 0, ret_in_w[:, :, bass.ds(h * RET_DK, RET_DK)])
                load(u + 1, 1, ret_in_w[:, :, bass.ds(h * RET_DK + D, RET_DK)])
                sp.dma_start(decay[:], A["decay"][:, bass.ds(h * PACKED, PACKED)]).then_inc(decay_in, 16)
                for j in range(2):
                    load(u + 2 + j, j, ret_in_w[:, 4 * j:4 * j + 4, bass.ds(h * RET_DV + 2 * D, RET_DV)])
                for j in range(2):
                    load(u + 4 + j, j, ret_in_w[:, 4 * j:4 * j + 4, bass.ds(h * RET_DV + 4 * D, RET_DV)])

            def closing(c):
                u0 = CLOSERS[c][0]

                def step(i, par):
                    load(u0 + i, (u0 + par) % 2, close_w[c][:, bass.ds(2 * i, 2), :])

                step(0, 0)
                gain = A["norm_gains"][c // 2]
                sp.wait_ge(pre_scaled, ST * (c + 1))
                if c:
                    sp.wait_ge(post_scaled, ST * c)
                else:
                    sp.wait_ge(qk_split, 2 * RET_HEADS)
                sp.dma_start(g_post[:], spread(gain[2 * (c % 2) + 1], D)).then_inc(gpost_in, 16)
                if c < 3:
                    nxt = A["norm_gains"][(c + 1) // 2][2 * ((c + 1) % 2)]
                    sp.dma_start(g_pre[:], spread(nxt, D)).then_inc(gpre_in, 16)
                n = CLOSERS[c][1]
                pairs = (n - 2) // 2
                with sp.Fori(0, pairs) as i:
                    for j in (1, 2):
                        step(2 * i + j, j)
                for u in range(1 + 2 * pairs, n):
                    step(u, u)

            def gate_up(l):
                with sp.Fori(0, FFN_N) as i:
                    u = GU_U[l] + 2 * i
                    load(u, GU_U[l] % 2, gate_w[l][:, :, bass.ds(i * 256, 256)])
                    load(u + 1, (GU_U[l] + 1) % 2, up_w[l][:, :, bass.ds(i * 256, 256)])

            def group_units(g):
                u = DIFF_U + DIFF_N * g
                load(u, DIFF_U % 2, diff_in_w[:, :, bass.ds(g * 256, 256)])
                load(u + 1, (DIFF_U + 1) % 2, diff_in_w[:, :, bass.ds(g * 256 + D, 256)])
                for j in range(2):
                    load(u + 2 + j, (DIFF_U + j) % 2, diff_in_w[:, 4 * j:4 * j + 4, bass.ds(g * 256 + 2 * D, 256)])

            def bias_tile(head, j):
                src = bias_tiles[bass.ds(head, 1)].rearrange("a p s -> (a p) s")
                sp.dma_start(nbias[j][:], src).then_inc(nbias_in[j], 16)

            closing(0)
            gate_up(0)
            closing(1)
            group_units(0)
            sp.wait_ge(a_split, CLOSER_BASE[2])
            sp.wait_ge(bias_spread, 16)
            for j in range(GROUP):
                bias_tile(j, j)
            with sp.Fori(1, GROUPS) as g:
                group_units(g)
                for j in range(GROUP):
                    sp.wait_ge(lg_made, 8 * (2 * g - 1 + j))
                    bias_tile(2 * g + j, j)
            closing(2)
            gate_up(1)
            closing(3)
            for t in range(ST):
                sp.wait_ge(x_added, 3 * ST + t + 1)
                sp.dma_start(out[0, t * P:(t + 1) * P, :], x[:, t, :]).then_inc(out_done, 16)
            sp.wait_ge(out_done, 16 * ST)

        @block.gpsimd
        def _(pool):
            nc.gpsimd.memset(expo[:], -0.5).then_inc(set_up, 1)
            nc.gpsimd.memset(eps[:], EPS).then_inc(set_up, 1)
            pool.wait_ge(set_up, 3)

            def rsqrt(mean_sq, ms_sem, ms_n, out_ap, done, cols):
                nc.gpsimd.tensor_tensor(out_ap, mean_sq, eps[:, 0:cols], ALU.add).then_inc(ms_sem, 1)
                pool.wait_ge(ms_sem, ms_n)
                nc.gpsimd.tensor_tensor(out_ap, out_ap, expo[:, 0:cols], ALU.pow).then_inc(done, 1)

            def pre(c, t):
                pool.wait_ge(pre_ssq, ST * c + t + 1)
                rsqrt(ssq[:, 4 + t:5 + t], pre_ms, ST * c + t + 1, rstd[:, 4 + t:5 + t], pre_rstd, 1)

            def post(c, t):
                pool.wait_ge(post_ssq, ST * c + t + 1)
                rsqrt(ssq[:, t:t + 1], post_ms, ST * c + t + 1, rstd[:, t:t + 1], post_rstd, 1)
                pool.wait_ge(post_scaled, ST * c + t + 1)
                nc.gpsimd.tensor_tensor(x[:, t, :], x[:, t, :], tmp[:, t % 2, :], ALU.add).then_inc(x_added, 1)

            def boundary(c):
                for t in range(ST + 1):
                    if t < ST:
                        post(c, t)
                    if t >= 1 and c < 3:
                        pre(c + 1, t - 1)

            for t in range(ST):
                pre(0, t)
            with pool.Fori(0, RET_HEADS) as h:
                pool.wait_ge(ret_ssq, ST * h + ST)
                rsqrt(ssq[:, 8:12], ret_ms, h + 1, rstd[:, 8:12], ret_rstd, ST)
            boundary(0)
            boundary(1)

            def attention(head):
                for t in range(ST):
                    if t == 0:
                        pool.wait_ge(lam_scaled, head + 1)
                    e1 = lg[:, 1, OFF[t]:OFF[t] + (t + 1) * P]
                    nc.gpsimd.tensor_tensor(e1, e1, stat[:, 20 + t:21 + t].to_broadcast([P, (t + 1) * P]),
                                            ALU.mult).then_inc(e1_scaled, 1)

            def o_norm(head):
                pool.wait_ge(o_ssq, head + 1)
                rsqrt(stat[:, 24:28], o_ms, head + 1, stat[:, 28:32], o_rstd, ST)

            with pool.Fori(0, GROUPS) as g:
                for j in range(GROUP):
                    attention(2 * g + j)
                for j in range(GROUP):
                    o_norm(2 * g + j)
            boundary(2)
            boundary(3)

        @block.scalar
        def _(act):
            for t in range(ST):
                act.dma_start(x[:, t, :], A["x"][0, t * P:(t + 1) * P, :]).then_inc(x_in[t], 16)
            act.dma_start(ident[:], A["ident"]).then_inc(const_in, 16)
            act.dma_start(g_pre[:], spread(A["norm_gains"][0][0], D)).then_inc(gpre_in, 16)
            act.dma_start(cs[:], A["cos_sin"]).then_inc(cs_in, 16)
            act.dma_start(rel[0:BUCKETS, :], A["rel_bias_table"]).then_inc(rel_in, 16)
            act.dma_start(tmp[0:BUCKETS + 1, 0, 0:640], A["buckets"]).then_inc(rel_in, 16)
            lam_tile = tmp[:, 1, 640:640 + 4 * DIFF_DH]
            act.dma_start(lam_tile, spread(A["diff_lambda"][0][0], 4 * DIFF_DH)).then_inc(lam_in, 16)
            act.dma_start(subg[:, 0:1], A["diff_subln"].rearrange("a (d b) -> (a d) b", b=1)).then_inc(lam_in, 16)

            def prep(u, slot, size=UNIT):
                act.wait_ge(w_used, u - 1 + PRIME)
                act.wait_ge(raw_in[slot], 8 * (u - slot) + 16)
                nc.scalar.activation(w_hi[slot][:, 0:size], raw[slot][:, 0:size], ACT.Copy).then_inc(w_hi_made, 1)

            def mean_square(src, col, done, before):
                for s, count in before:
                    if isinstance(count, int) and count == 0:
                        continue
                    act.wait_ge(s, count)
                n = src.shape[-1]
                nc.scalar.activation(junk[:, 0:n], src, ACT.Square, scale=n ** -0.5, accum_out=ssq[:, col:col + 1]).then_inc(done, 1)

            def pre_square(c, t):
                if c == 0:
                    act.wait_ge(x_in[t], 16)
                else:
                    act.wait_ge(x_added, ST * (c - 1) + t + 1)
                before = [(pre_ssq, ST * c + t)]
                if c:
                    before.append((post_ssq, ST * (c - 1) + min(t + 2, ST)))
                mean_square(x[:, t, :], 4 + t, pre_ssq, before)

            def pre_high(c, t):
                act.wait_ge(pre_turned, ST * c + t + 1)
                nc.scalar.activation(h_hi[:, :, t * P:(t + 1) * P],
                                     bank(2 * t, 2).rearrange("p (k s) -> p k s", k=KT), ACT.Copy).then_inc(h_hi_made, 1)

            def boundary(c):
                u_end = CLOSERS[c][0] + CLOSERS[c][1]
                for t in range(ST + 2):
                    if t < ST:
                        if t < ST - 1:
                            act.wait_ge(row_done, (ST - 1) * c + t + 1)
                        else:
                            act.wait_ge(w_used, u_end + PRIME)
                        mean_square(bank(2 * t, 2), t, post_ssq,
                                    [(post_ssq, ST * c + t), (pre_ssq, ST * (c + 1) + (max(t - 1, 0) if c < 3 else 0))])
                    if 1 <= t <= ST and c < 3:
                        pre_square(c + 1, t - 1)
                    if t >= 2 and c < 3:
                        pre_high(c + 1, t - 2)

            def a_high(c, i, slot):
                src = (yT, hidden, oT, hidden)[c]
                nc.scalar.activation(h_hi[:, 2 * slot:2 * slot + 2, :], src[:, bass.ds(2 * i, 2), :],
                                     ACT.Copy).then_inc(a_hi_made, 1)

            def closing(c):
                u0, n = CLOSERS[c]
                act.wait_ge(w_used, u0 + PRIME)
                if c % 2:
                    act.wait_ge(hid_made, 1 + FFN_N * (c // 2 + 1))
                a_high(c, 0, u0 % 2)

                def step(i, par):
                    last = isinstance(i, int) and i == n - 1
                    if not (last and c == 3):
                        prep(u0 + i + 1, (u0 + par + 1) % 2)
                    if not last:
                        a_high(c, i + 1, (u0 + par + 1) % 2)

                closing_steps(c, step, act)
                boundary(c)

            def gate_up(l):
                with act.Fori(0, FFN_N) as i:
                    u = GU_U[l] + 2 * i
                    prep(u + 1, (GU_U[l] + 1) % 2)
                    act.wait_ge(w_used, u + 1 + PRIME)
                    act.wait_ge(hid_made, 1 + FFN_N * l + i)
                    nc.scalar.activation(sil[:], bank(0, 2).rearrange("p (a s) -> p a s", a=2), ACT.Silu)\
                        .then_inc(sil_made, 1)
                    prep(u + 2, GU_U[l] % 2)

            for t in range(ST + 1):
                if t < ST:
                    pre_square(0, t)
                if t >= 1:
                    pre_high(0, t - 1)
                if t == 1:
                    prep(0, 0)
            act.wait_ge(lam_sum, 2)
            nc.scalar.activation(lam[:, 2:4], lam[:, 0:2], ACT.Exp).then_inc(lam_exp, 1)
            act.wait_ge(bias_cp, 1)
            act.dma_start(bias_rows, tmp[0:DIFF_HEADS, 1, 0:640]).then_inc(bias_stored, 16)
            act.wait_ge(bias_stored, 16)
            diagonals = bass.AP(tensor=bias_rows.tensor, offset=bias_rows.offset + P - 1, ap=[[640, DIFF_HEADS], [-1, P], [1, S]])
            act.dma_start(bias_tiles, diagonals).then_inc(bias_spread, 16)

            with act.Fori(0, RET_HEADS) as h:
                u = RET_U + RET_N * h
                for j in range(2):
                    prep(u + 1 + j, (1 + j) % 2)
                    act.wait_ge(rot_made, 2 * h + 1 + j)
                    nc.scalar.activation(qk_hi[:, 2 * j:2 * j + 2, :], tmp[:, 0, :].rearrange("p (a s) -> p a s", a=2),
                                         ACT.Copy).then_inc(qk_hi_made, 1)
                prep(u + 3, 1)
                prep(u + 4, 0)
                act.wait_ge(inner_made, h + 1)
                nc.scalar.activation(in_hi[:], tmp[:].rearrange("p a d -> p (a d)")[:, 0:PACKED],
                                     ACT.Copy).then_inc(inner_hi_made, 1)
                for t in range(ST):
                    if t < ST - 1:
                        act.wait_ge(rv_row, (ST - 1) * h + t + 1)
                    else:
                        act.wait_ge(w_used, u + 4 + PRIME)
                    nc.scalar.activation(rv_hi[:, t, :], bank(4 + t), ACT.Copy).then_inc(rv_hi_made, 1)
                prep(u + 5, 1)
                for t in range(ST):
                    act.wait_ge(ret_mm, ST * h + t + 1)
                    mean_square(bank(t), 8 + t, ret_ssq, [(ret_ssq, ST * h + t)] if t else [])
                prep(u + 6, 0)
                for t in range(ST):
                    if t < ST - 1:
                        act.wait_ge(gate_row, (ST - 1) * h + t + 1)
                    else:
                        act.wait_ge(w_used, u + 6 + PRIME)
                    nc.scalar.activation(gated[:, t, :], bank(4 + t), ACT.Silu).then_inc(gate_made, 1)
                for t in range(ST):
                    act.wait_ge(y_turned, ST * h + t + 1)
                    nc.scalar.activation(yT[:, bass.ds(4 * h, 4), t * P:(t + 1) * P],
                                         bank(t).rearrange("p (a s) -> p a s", a=4), ACT.Copy).then_inc(yT_made, 1)
            closing(0)
            gate_up(0)
            closing(1)

            def units_q(g, j):
                nc.scalar.activation(q_hi[:, j, :], bank(5 + j), ACT.Copy, scale=-(DIFF_DH ** -0.5)).then_inc(q_hi_made, 1)

            def units_k(g):
                act.wait_ge(w_used, DIFF_U + DIFF_N * g + 2 + PRIME)
                for j in range(GROUP):
                    nc.scalar.activation(k_hi[:, j, :], bank(5 + j), ACT.Copy).then_inc(k_hi_made, 1)

            def units_v(g):
                act.wait_ge(w_used, DIFF_U + DIFF_N * g + 4 + PRIME)
                for t in range(ST):
                    nc.scalar.activation(v_hi[:, t, :], bank(t)[:, 0:256], ACT.Copy).then_inc(v_hi_made, 1)

            def exps(head):
                for n, (t, i) in enumerate(ORDER):
                    act.wait_ge(lg_made, 8 * head + n + 1)
                    e = lg[:, i, OFF[t]:OFF[t] + (t + 1) * P]
                    nc.scalar.activation(e, e, ACT.Exp, bias=stat[:, 4 * i + t:4 * i + t + 1], scale=-1.0,
                                         accum_out=stat[:, 8 + 4 * i + t:9 + 4 * i + t]).then_inc(exp_made, 1)

            def aT_high(head):
                act.wait_ge(a_turned, head + 1)
                nc.scalar.activation(aT_hi[:], ps[:, 0:PACKED], ACT.Copy).then_inc(aT_hi_made, 1)

            def o_square(head, j):
                act.wait_ge(o_mm, head + 1)
                nc.scalar.activation(o_n[j][:], bank((7, 4)[j]).rearrange("p (a d) -> p a d", a=ST),
                                     ACT.Square, scale=DIFF_DV ** -0.5).then_inc(o_sq, 1)

            def oT_copy(head, j):
                act.wait_ge(o_turned, head + 1)
                nc.scalar.activation(oT[:, bass.ds(head, 1), :].rearrange("p a s -> p (a s)"), bank(5 + j), ACT.Copy,
                                     scale=subg[:, 1:2]).then_inc(oT_made, 1)

            s0, s1 = DIFF_U % 2, (DIFF_U + 1) % 2
            half = UNIT // 2
            prep(DIFF_U + 1, s1)
            act.wait_ge(w_used, DIFF_U + 1 + PRIME)
            for j in range(GROUP):
                units_q(0, j)
            prep(DIFF_U + 2, s0, half)
            units_k(0)
            prep(DIFF_U + 3, s1, half)
            prep(DIFF_U + 4, s0)
            units_v(0)
            with act.Fori(1, GROUPS) as g:
                u = DIFF_U + DIFF_N * g
                head = 2 * g - 2
                prep(u + 1, s1)
                exps(head)
                act.wait_ge(w_used, u + 1 + PRIME)
                units_q(g, 0)
                aT_high(head)
                prep(u + 2, s0, half)
                act.wait_ge(qk_mm, head + 2)
                units_q(g, 1)
                exps(head + 1)
                units_k(g)
                aT_high(head + 1)
                prep(u + 3, s1, half)
                o_square(head, 0)
                o_square(head + 1, 1)
                prep(u + 4, s0)
                units_v(g)
                oT_copy(head, 0)
                oT_copy(head + 1, 1)
            head = DIFF_HEADS - GROUP
            for j in range(GROUP):
                exps(head + j)
                aT_high(head + j)
            for j in range(GROUP):
                o_square(head + j, j)
            for j in range(GROUP):
                oT_copy(head + j, j)
            closing(2)
            gate_up(1)
            closing(3)

        @block.vector
        def _(dve):
            nc.vector.memset(rel[BUCKETS:BUCKETS + 1, :], MASKED).then_inc(set_up, 1)
            dve.sem_inc(w_split, PRIME)
            dve.sem_inc(w_used, PRIME)
            dve.sem_inc(hid_made, 1)
            dve.sem_inc(yT_made, ST)
            dve.sem_inc(oT_made, 1)

            def low(out_ap, whole, high, done):
                nc.vector.tensor_tensor(out_ap, whole, high.bitcast(F32), ALU.subtract).then_inc(done, 1)

            def prep(u, slot, size=UNIT):
                dve.wait_ge(w_hi_made, u + 1)
                low(w_lo[slot][:, 0:size], raw[slot][:, 0:size], w_hi[slot][:, 0:size], w_split)

            def pre_scale(c, t):
                dve.wait_ge(pre_rstd, ST * c + t + 1)
                if t == 0:
                    dve.wait_ge(gpre_in, 16 * (c + 1))
                if t >= 1:
                    dve.wait_ge(pre_turned, ST * c + t)
                nc.vector.scalar_tensor_tensor(out=tmp[:, 2, :], in0=x[:, t, :], scalar=rstd[:, 4 + t:5 + t],
                                               in1=g_pre[:], op0=ALU.mult, op1=ALU.mult).then_inc(pre_scaled, 1)

            def pre_low(c, t):
                dve.wait_ge(h_hi_made, ST * c + t + 1)
                low(h_lo[:, :, t * P:(t + 1) * P], bank(2 * t, 2).rearrange("p (k s) -> p k s", k=KT),
                    h_hi[:, :, t * P:(t + 1) * P], h_split)

            def boundary(c):
                for t in range(ST + 2):
                    if t < ST:
                        dve.wait_ge(post_rstd, ST * c + t + 1)
                        if t == 0:
                            dve.wait_ge(gpost_in, 16 * (c + 1))
                        if t >= 2:
                            dve.wait_ge(x_added, ST * c + t - 1)
                        nc.vector.scalar_tensor_tensor(out=tmp[:, t % 2, :], in0=bank(2 * t, 2),
                                                       scalar=rstd[:, t:t + 1], in1=g_post[:],
                                                       op0=ALU.mult, op1=ALU.mult).then_inc(post_scaled, 1)
                    if 1 <= t <= ST and c < 3:
                        pre_scale(c + 1, t - 1)
                    if t >= 2 and c < 3:
                        pre_low(c + 1, t - 2)

            def a_low(c, i, slot):
                src = (yT, hidden, oT, hidden)[c]
                dve.wait_ge(a_hi_made, CLOSER_BASE[c] + i + 1)
                low(h_lo[:, 2 * slot:2 * slot + 2, :], src[:, bass.ds(2 * i, 2), :],
                    h_hi[:, 2 * slot:2 * slot + 2, :], a_split)

            def closing(c):
                u0, n = CLOSERS[c]
                a_low(c, 0, u0 % 2)

                def step(i, par):
                    last = isinstance(i, int) and i == n - 1
                    if not (last and c == 3):
                        prep(u0 + i + 1, (u0 + par + 1) % 2)
                    if not last:
                        a_low(c, i + 1, (u0 + par + 1) % 2)

                closing_steps(c, step, dve)
                boundary(c)

            def gate_up(l):
                with dve.Fori(0, FFN_N) as i:
                    u = GU_U[l] + 2 * i
                    prep(u + 1, (GU_U[l] + 1) % 2)
                    prep(u + 2, GU_U[l] % 2)
                    dve.wait_ge(sil_made, FFN_N * l + i + 1)
                    dve.wait_ge(w_used, u + 2 + PRIME)
                    nc.vector.tensor_tensor(hidden[:, bass.ds(2 * i, 2), :], sil[:],
                                            bank(2, 2).rearrange("p (a s) -> p a s", a=2), ALU.mult)\
                        .then_inc(hid_made, 1)

            for t in range(ST + 1):
                if t < ST:
                    pre_scale(0, t)
                if t >= 1:
                    pre_low(0, t - 1)
                if t == 1:
                    prep(0, 0)
            dve.wait_ge(lam_in, 32)
            lt = tmp[:, 1, 640:640 + 4 * DIFF_DH]
            for i in range(2):
                a, b = lt[:, 128 * i:128 * i + 64], lt[:, 128 * i + 64:128 * i + 128]
                nc.vector.tensor_tensor_reduce(out=junk[:, 64 * i:64 * i + 64],
                                               in0=a, in1=b, scale=1.0, scalar=0.0,
                                               op0=ALU.mult, op1=ALU.add, accum_out=lam[:, i:i + 1]).then_inc(lam_sum, 1)
            dve.wait_ge(lam_exp, 1)
            nc.vector.tensor_tensor(lam[:, 4:5], lam[:, 3:4], lam[:, 2:3], ALU.subtract).then_inc(lam_made, 1)
            nc.vector.tensor_scalar(subg[:, 1:2], subg[:, 0:1], 1.0 - LAMBDA_INIT, None, ALU.mult).then_inc(lam_made, 1)
            dve.wait_ge(lam_made, 2)
            nc.vector.tensor_scalar(lam[:, 5:6], lam[:, 4:5], -LAMBDA_INIT, None, ALU.add).then_inc(lam_made, 1)
            dve.wait_ge(bias_mm, 1)
            nc.vector.tensor_copy(tmp[0:DIFF_HEADS, 1, 0:640], ps[0:DIFF_HEADS, 0:640]).then_inc(bias_cp, 1)
            dve.wait_ge(bias_stored, 16)
            dve.wait_ge(cs_in, 16)
            with dve.Fori(0, RET_HEADS) as h:
                u = RET_U + RET_N * h
                ac = tmp[:, 0, :].rearrange("p (a s) -> p a s", a=2)
                bd = tmp[:, 1, :].rearrange("p (a s) -> p a s", a=2)
                for j in range(2):
                    prep(u + 1 + j, (1 + j) % 2)
                    dve.wait_ge(w_used, u + 1 + j + PRIME)
                    if j:
                        dve.wait_ge(qk_split, 2 * h + 1)
                    x1, x2 = bank(2 * j), bank(2 * j + 1)
                    nc.vector.tensor_tensor(ac[:, 0, :], x1, cs[:, 0, :], ALU.mult)
                    nc.vector.tensor_tensor(bd[:, 0, :], x2, cs[:, 1, :], ALU.mult)
                    nc.vector.tensor_tensor(ac[:, 1, :], x1, cs[:, 1, :], ALU.mult)
                    nc.vector.tensor_tensor(bd[:, 1, :], x2, cs[:, 0, :], ALU.mult).then_inc(rot_mul, 1)
                    dve.wait_ge(rot_mul, 2 * h + 1 + j)
                    nc.vector.tensor_tensor(ac[:, 0, :], ac[:, 0, :], bd[:, 0, :], ALU.subtract)
                    nc.vector.tensor_tensor(ac[:, 1, :], ac[:, 1, :], bd[:, 1, :], ALU.add).then_inc(rot_made, 1)
                    dve.wait_ge(qk_hi_made, 2 * h + 1 + j)
                    low(qk_lo[:, 2 * j:2 * j + 2, :], ac, qk_hi[:, 2 * j:2 * j + 2, :], qk_split)
                prep(u + 3, 1)
                prep(u + 4, 0)
                dve.wait_ge(inner_mm, h + 1)
                dve.wait_ge(decay_in, 16 * h + 16)
                inner = tmp[:].rearrange("p a d -> p (a d)")[:, 0:PACKED]
                nc.vector.tensor_tensor(inner, ps[:, 0:PACKED], decay[:], ALU.mult).then_inc(inner_made, 1)
                dve.wait_ge(inner_hi_made, h + 1)
                low(in_lo[:], inner, in_hi[:], inner_split)
                for t in range(ST):
                    dve.wait_ge(rv_hi_made, ST * h + t + 1)
                    low(rv_lo[:, t, :], bank(4 + t), rv_hi[:, t, :], rv_split)
                prep(u + 5, 1)
                prep(u + 6, 0)
                dve.wait_ge(ret_rstd, h + 1)
                for t in range(ST):
                    dve.wait_ge(gate_made, ST * h + t + 1)
                    nc.vector.scalar_tensor_tensor(out=gated[:, t, :], in0=bank(t), scalar=rstd[:, 8 + t:9 + t],
                                                   in1=gated[:, t, :], op0=ALU.mult, op1=ALU.mult).then_inc(y_made, 1)
            closing(0)
            gate_up(0)
            closing(1)

            def units_q(g, j):
                dve.wait_ge(q_hi_made, 2 * g + j + 1)
                nc.vector.scalar_tensor_tensor(out=q_lo[:, j, :], in0=bank(5 + j), scalar=-(DIFF_DH ** -0.5),
                                               in1=q_hi[:, j, :].bitcast(F32), op0=ALU.mult,
                                               op1=ALU.subtract).then_inc(q_split, 1)

            def units_k(g):
                for j in range(GROUP):
                    dve.wait_ge(k_hi_made, 2 * g + j + 1)
                    low(k_lo[:, j, :], bank(5 + j), k_hi[:, j, :], k_split)

            def units_v(g):
                for t in range(ST):
                    dve.wait_ge(v_hi_made, ST * g + t + 1)
                    low(v_lo[:, t, :], bank(t)[:, 0:256], v_hi[:, t, :], v_split)

            def logits(head, j, unit=None):
                dve.wait_ge(qk_mm, head + 1)
                dve.wait_ge(nbias_in[j], 8 * (head - j) + 16)
                if unit:
                    prep(*unit)
                for t, i in ORDER:
                    n = (t + 1) * P
                    nc.vector.tensor_tensor_reduce(out=lg[:, i, OFF[t]:OFF[t] + n], in0=scores(t, i),
                                                   in1=nbias[j][:, S - n:S], scale=1.0, scalar=3e38,
                                                   op0=ALU.add, op1=ALU.min,
                                                   accum_out=stat[:, 4 * i + t:4 * i + t + 1]).then_inc(lg_made, 1)

            def attn(head):
                dve.wait_ge(exp_made, 8 * head + 8)
                nc.vector.reciprocal(stat[:, 16:24], stat[:, 8:16]).then_inc(recip_made, 1)
                dve.wait_ge(recip_made, head + 1)
                nc.vector.tensor_scalar(stat[:, 20:24], stat[:, 20:24], lam[:, 5:6], None, ALU.mult).then_inc(lam_scaled, 1)
                for t in range(ST):
                    dve.wait_ge(e1_scaled, ST * head + t + 1)
                    n = (t + 1) * P
                    e0, e1 = (lg[:, i, OFF[t]:OFF[t] + n] for i in range(2))
                    nc.vector.scalar_tensor_tensor(out=e0, in0=e0, scalar=stat[:, 16 + t:17 + t], in1=e1,
                                                   op0=ALU.mult, op1=ALU.add).then_inc(attn_made, 1)

            def aT_low(head):
                dve.wait_ge(aT_hi_made, head + 1)
                low(aT_lo[:], ps[:, 0:PACKED], aT_hi[:], aT_split)

            def o_norm(head, j):
                dve.wait_ge(o_sq, head + 1)
                nc.vector.tensor_reduce(stat[:, 24:28], o_n[j][:], AX_X, ALU.add).then_inc(o_ssq, 1)
                dve.wait_ge(o_rstd, head + 1)
                nc.vector.tensor_tensor(o_n[j][:], bank((7, 4)[j]).rearrange("p (a d) -> p a d", a=ST),
                                        stat[:, 28:32].unsqueeze(2).to_broadcast([P, ST, P]), ALU.mult)\
                    .then_inc(o_normed, 1)

            s0, s1 = DIFF_U % 2, (DIFF_U + 1) % 2
            half = UNIT // 2
            prep(DIFF_U + 1, s1)
            for j in range(GROUP):
                units_q(0, j)
            prep(DIFF_U + 2, s0, half)
            units_k(0)
            prep(DIFF_U + 3, s1, half)
            prep(DIFF_U + 4, s0)
            units_v(0)
            with dve.Fori(1, GROUPS) as g:
                u = DIFF_U + DIFF_N * g
                head = 2 * g - 2
                logits(head, 0, (u + 1, s1))
                attn(head)
                units_q(g, 0)
                aT_low(head)
                logits(head + 1, 1, (u + 2, s0, half))
                units_q(g, 1)
                attn(head + 1)
                units_k(g)
                aT_low(head + 1)
                prep(u + 3, s1, half)
                o_norm(head, 0)
                o_norm(head + 1, 1)
                prep(u + 4, s0)
                units_v(g)
            head = DIFF_HEADS - GROUP
            for j in range(GROUP):
                logits(head + j, j)
                attn(head + j)
                aT_low(head + j)
            for j in range(GROUP):
                o_norm(head + j, j)
            closing(2)
            gate_up(1)
            closing(3)

        @block.tensor
        def _(pe):
            def three(out_ap, a_hi, a_lo, b_hi, b_lo, start, stop):
                nc.tensor.matmul(out_ap, a_hi, b_hi, start=start, stop=False)
                nc.tensor.matmul(out_ap, a_hi, b_lo, start=False, stop=False)
                return nc.tensor.matmul(out_ap, a_lo, b_hi, start=False, stop=stop)

            def columns(u, slot, first_bank, before=None):
                pe.wait_ge(w_split, u + 1 + PRIME)
                wh, wl = (w[slot][:].rearrange("p (k n) -> p k n", k=KT) for w in (w_hi, w_lo))
                for m in range(2):
                    if before:
                        before(m)
                    at = slice(m * P, (m + 1) * P)
                    for k in range(KT):
                        mm = three(bank(first_bank + m), wh[:, k, at], wl[:, k, at], h_hi[:, k, :], h_lo[:, k, :],
                                   k == 0, k == KT - 1)
                mm.then_inc(w_used, 1)

            def rows(u, slot, j, first_bank, n, row_sem):
                pe.wait_ge(w_split, u + 1 + PRIME)
                wh, wl = (w[slot][:, 0:4 * n].rearrange("p (k n) -> p k n", k=4) for w in (w_hi, w_lo))
                for t in range(ST):
                    for k in range(4):
                        kk = 4 * j + k
                        at = slice(t * P, (t + 1) * P)
                        mm = three(bank(first_bank + t)[:, 0:n], h_hi[:, kk, at], h_lo[:, kk, at], wh[:, k, :], wl[:, k, :],
                                   kk == 0, kk == KT - 1)
                    if j and t < ST - 1 and row_sem is not None:
                        mm.then_inc(row_sem, 1)
                mm.then_inc(w_used, 1)

            def closing(c):
                u0, n = CLOSERS[c]

                def step(i, par):
                    slot = (u0 + par) % 2
                    first, last = (isinstance(i, int) and i == e for e in (0, n - 1))
                    pe.wait_ge(w_split, u0 + i + 1 + PRIME)
                    pe.wait_ge(a_split, CLOSER_BASE[c] + i + 1)
                    wh, wl = (w[slot][:].rearrange("p (k n) -> p k n", k=2) for w in (w_hi, w_lo))
                    for t in range(ST):
                        for k in range(2):
                            kk, at = 2 * slot + k, slice(t * P, (t + 1) * P)
                            for half in range(2):
                                cols = slice(half * BANK, (half + 1) * BANK)
                                mm = three(bank(2 * t + half), h_hi[:, kk, at], h_lo[:, kk, at],
                                           wh[:, k, cols], wl[:, k, cols], first and k == 0, last and k == 1)
                        if last and t < ST - 1:
                            mm.then_inc(row_done, 1)
                    mm.then_inc(w_used, 1)

                closing_steps(c, step, pe)
                if c < 3:
                    for t in range(ST):
                        turn_rows(c + 1, t)

            def turn_rows(c, t):
                pe.wait_ge(pre_scaled, ST * c + t + 1)
                for k in range(KT):
                    mm = nc.tensor.transpose(ps[:, 2 * t * BANK + k * P:2 * t * BANK + (k + 1) * P],
                                             tmp[:, 2, k * P:(k + 1) * P], ident[:])
                mm.then_inc(pre_turned, 1)

            def gate_up(l):
                pe.wait_ge(h_split, ST * (2 * l + 2))
                with pe.Fori(0, FFN_N) as i:
                    u = GU_U[l] + 2 * i
                    columns(u, GU_U[l] % 2, 0)
                    pe.wait_ge(hid_made, 1 + FFN_N * l + i)
                    columns(u + 1, (GU_U[l] + 1) % 2, 2)
                    pe.wait_ge(sil_made, FFN_N * l + i + 1)
                pe.wait_ge(hid_made, 1 + FFN_N * (l + 1))

            pe.wait_ge(const_in, 16)
            for t in range(ST):
                turn_rows(0, t)
            pe.wait_ge(h_split, ST)
            pe.wait_ge(rel_in, 32)
            pe.wait_ge(set_up, 3)
            nc.tensor.matmul(ps[0:DIFF_HEADS, 0:BANK], rel[:], tmp[0:BUCKETS + 1, 0, 0:BANK], start=True, stop=True)
            nc.tensor.matmul(ps[0:DIFF_HEADS, BANK:640], rel[:], tmp[0:BUCKETS + 1, 0, BANK:640],
                             start=True, stop=True).then_inc(bias_mm, 1)
            pe.wait_ge(bias_cp, 1)
            with pe.Fori(0, RET_HEADS) as h:
                u = RET_U + RET_N * h
                pe.wait_ge(yT_made, ST * h + ST)
                columns(u, 0, 0)
                columns(u + 1, 1, 2)
                rows(u + 2, 0, 0, 4, RET_DV, None)
                pe.wait_ge(qk_split, 2 * h + 2)
                for m in (0, 1, 3, 2):
                    n = (ST - m) * P
                    at = OFF[ST - 1 - m]
                    for d in range(2):
                        ks = slice(m * P, (m + 1) * P)
                        mm = three(ps[:, at:at + n], qk_hi[:, 2 + d, ks], qk_lo[:, 2 + d, ks],
                                   qk_hi[:, d, m * P:S], qk_lo[:, d, m * P:S], d == 0, d == 1)
                mm.then_inc(inner_mm, 1)
                rows(u + 3, 1, 1, 4, RET_DV, rv_row)
                pe.wait_ge(inner_split, h + 1)
                for t in range(ST):
                    pe.wait_ge(rv_split, ST * h + t + 1)
                    for m in range(t + 1):
                        at = OFF[ST - 1 - m] + (t - m) * P
                        mm = three(bank(t), in_hi[:, at:at + P], in_lo[:, at:at + P], rv_hi[:, m, :], rv_lo[:, m, :],
                                   m == 0, m == t)
                    mm.then_inc(ret_mm, 1)
                rows(u + 4, 0, 0, 4, RET_DV, None)
                rows(u + 5, 1, 1, 4, RET_DV, gate_row)
                for t in range(ST):
                    pe.wait_ge(y_made, ST * h + t + 1)
                    for a in range(4):
                        mm = nc.tensor.transpose(ps[:, t * BANK + a * P:t * BANK + (a + 1) * P],
                                                 gated[:, t, a * P:(a + 1) * P], ident[:])
                    mm.then_inc(y_turned, 1)
            pe.wait_ge(yT_made, ST * RET_HEADS + ST)
            closing(0)
            gate_up(0)
            closing(1)

            def attention_scores(head, j):
                pe.wait_ge(q_split, head + 1)
                pe.wait_ge(k_split, head + 1)
                for t, i in ORDER:
                    d = slice(DIFF_DH * i, DIFF_DH * (i + 1))
                    if (t, i) == (1, 1):
                        pe.wait_ge(shared_bank, head + 1)
                    mm = three(scores(t, i), q_hi[d, j, t * P:(t + 1) * P], q_lo[d, j, t * P:(t + 1) * P],
                               k_hi[d, j, 0:(t + 1) * P], k_lo[d, j, 0:(t + 1) * P], True, True)
                    if (t, i) == (1, 0):
                        mm.then_inc(shared_bank, 1)
                mm.then_inc(qk_mm, 1)

            def attention_out(head, j):
                for t in range(ST):
                    pe.wait_ge(attn_made, ST * head + t + 1)
                    for k in range(t + 1):
                        at = slice(OFF[t] + k * P, OFF[t] + (k + 1) * P)
                        mm = nc.tensor.transpose(ps[:, at], lg[:, 0, at], ident[:])
                mm.then_inc(a_turned, 1)
                pe.wait_ge(aT_split, head + 1)
                for t in range(ST):
                    o = bank((7, 4)[j])[:, t * P:(t + 1) * P]
                    for k in range(t + 1):
                        at = slice(OFF[t] + k * P, OFF[t] + (k + 1) * P)
                        dv = slice(j * DIFF_DV, (j + 1) * DIFF_DV)
                        mm = three(o, aT_hi[:, at], aT_lo[:, at], v_hi[:, k, dv], v_lo[:, k, dv], k == 0, k == t)
                mm.then_inc(o_mm, 1)

            def turn_o(head, j):
                pe.wait_ge(o_normed, head + 1)
                for t in range(ST):
                    mm = nc.tensor.transpose(bank(5 + j)[:, t * P:(t + 1) * P], o_n[j][:, t, :], ident[:])
                mm.then_inc(o_turned, 1)

            s0, s1 = DIFF_U % 2, (DIFF_U + 1) % 2
            pe.wait_ge(h_split, 3 * ST)
            columns(DIFF_U, s0, 5)
            columns(DIFF_U + 1, s1, 5, before=lambda m: pe.wait_ge(q_split, m + 1))
            rows(DIFF_U + 2, s0, 0, 0, 256, None)
            rows(DIFF_U + 3, s1, 1, 0, 256, None)
            with pe.Fori(1, GROUPS) as g:
                u = DIFF_U + DIFF_N * g
                head = 2 * g - 2
                pe.wait_ge(v_split, ST * g)
                attention_scores(head, 0)
                pe.wait_ge(oT_made, head + 1)
                columns(u, s0, 5)
                attention_out(head, 0)
                attention_scores(head + 1, 1)
                columns(u + 1, s1, 5, before=lambda m: pe.wait_ge(q_split, 2 * g + m + 1))
                attention_out(head + 1, 1)
                rows(u + 2, s0, 0, 0, 256, None)
                rows(u + 3, s1, 1, 0, 256, None)
                for j in range(GROUP):
                    pe.wait_ge(k_split, 2 * g + j + 1)
                    turn_o(head + j, j)
            pe.wait_ge(v_split, ST * GROUPS)
            head = DIFF_HEADS - GROUP
            for j in range(GROUP):
                attention_scores(head + j, j)
                attention_out(head + j, j)
            pe.wait_ge(oT_made, head + 1)
            for j in range(GROUP):
                turn_o(head + j, j)
            pe.wait_ge(oT_made, DIFF_HEADS + 1)
            closing(2)
            gate_up(1)
            closing(3)


ORDER = [(1, 0), (3, 0), (3, 1), (2, 0), (2, 1), (0, 0), (0, 1), (1, 1)]


def constants():
    f32 = np.float32
    half = RET_DK // 2
    inv = f32(10000.0) ** (-np.arange(half, dtype=f32) / f32(half))
    ang = (np.arange(S, dtype=f32)[None, :] * inv[:, None]).astype(f32)
    cos_sin = np.stack([np.cos(ang), np.sin(ang)], 1).astype(f32)
    log_gamma = np.log1p(-(2.0 ** (-5.0 - np.arange(RET_HEADS))))
    decay = np.zeros((RET_HEADS, P, PACKED))
    key = np.arange(P)[:, None]
    for m in range(ST):
        n = (ST - m) * P
        d = np.arange(n)[None, :] - key
        at = OFF[ST - 1 - m]
        decay[:, :, at:at + n] = np.where(d >= 0, np.exp(np.maximum(d, 0) * log_gamma[:, None, None]), 0.0)
    decay = (decay * RET_DK ** -0.5).astype(f32).transpose(1, 0, 2).reshape(P, RET_HEADS * PACKED)
    dist = np.arange(S)
    exact = BUCKETS // 2
    large = exact + (np.log(np.maximum(dist, 1).astype(f32) / f32(exact)) / f32(np.log(128 / exact))
                     * f32(BUCKETS - exact)).astype(np.int32)
    bucket = np.where(dist < exact, dist, np.minimum(large, BUCKETS - 1))
    buckets = np.zeros((BUCKETS + 1, 640), f32)
    buckets[bucket[::-1], np.arange(S)] = -1.0
    buckets[BUCKETS, S:] = 1.0
    return {"cos_sin": cos_sin, "decay": np.ascontiguousarray(decay), "buckets": buckets, "ident": np.eye(P, dtype=f32)}


NAMES = ["x", "norm_gains", "ret_w_in", "ret_w_out", "diff_w_in", "diff_w_out", "diff_lambda", "diff_subln",
         "rel_bias_table", "ffn_w_gate", "ffn_w_up", "ffn_w_down"]


def kernel(**inputs):
    import concourse.bacc as bacc
    from concourse.bass_utils import run_bass_kernel_spmd

    nc = bacc.Bacc("TRN2", target_bir_lowering=False, num_devices=1)
    arrays, args = {}, {}
    for name, a in [*((n, inputs[n]) for n in NAMES), *constants().items()]:
        a = np.ascontiguousarray(a)
        arrays[f"in_{name}"] = a
        args[name] = nc.dram_tensor(f"in_{name}", a.shape, mybir.dt.from_np(a.dtype), kind="ExternalInput").ap()
    out = nc.dram_tensor("out", (1, S, D), F32, kind="ExternalOutput").ap()
    build(nc, args, out)
    r = run_bass_kernel_spmd(nc, [arrays], core_ids=[0])
    return r.results[0]["out"]
```

```python
from contextlib import ExitStack

import concourse.bass as bass
import numpy as np
from concourse import mybir

F32 = mybir.dt.float32
F32R = mybir.dt.float32r
BF16 = mybir.dt.bfloat16
ACT = mybir.ActivationFunctionType
ALU = mybir.AluOpType
AX_X = mybir.AxisListType.X

P = 128
S = 512
D = 1024
ST = S // P
KT = D // P
EPS = 1e-6
BANK = 512

RET_HEADS = 4
RET_DK = D // RET_HEADS
RET_DV = 2 * RET_DK

DIFF_HEADS = 8
DIFF_DH = D // (2 * DIFF_HEADS)
DIFF_DV = 2 * DIFF_DH
GROUP = 2
GROUPS = DIFF_HEADS // GROUP
LAMBDA_INIT = 0.8 - 0.6 * float(np.exp(-0.3))
BUCKETS = 32
MASKED = 1e30

D_FF = -(-8 * D // (3 * 256)) * 256
FT = D_FF // P

UNIT = 2048
HALF = UNIT // 2
PACKED = S + 384 + P + 256
RET_OFF = {3: 0, 2: 512, 0: 896, 1: 1024}
OFF = {1: 0, 3: 256, 2: 768, 0: 1152}

RET_N = 6
RETO_U = RET_N * RET_HEADS
RETO_N = RET_HEADS * RET_DV // (2 * P)
FFN_N = FT // 2
GU_U = [RETO_U + RETO_N, 0]
DN_U = [GU_U[0] + 2 * FFN_N, 0]
DIFF_U = DN_U[0] + FFN_N
DIFF_N = 4
DIFFO_U = DIFF_U + DIFF_N * GROUPS
DIFFO_N = KT // 2
GU_U[1] = DIFFO_U + DIFFO_N
DN_U[1] = GU_U[1] + 2 * FFN_N
CLOSERS = [(RETO_U, RETO_N), (DN_U[0], FFN_N), (DIFFO_U, DIFFO_N), (DN_U[1], FFN_N)]
CLOSER_BASE = [sum(n for _, n in CLOSERS[:c]) for c in range(4)]

PRIME = 2


def build(nc, A, out):
    bias_rows = nc.dram_tensor("bias_rows", (DIFF_HEADS, 640), F32, kind="Internal").ap()
    bias_tiles = nc.dram_tensor("bias_tiles", (DIFF_HEADS, P, S), F32, kind="Internal").ap()

    with ExitStack() as ctx:
        def sb(name, shape, dt=F32, within=ctx):
            return within.enter_context(nc.sbuf_tensor(name, shape, dt))

        def sem(name):
            return ctx.enter_context(nc.semaphore(name))

        x = sb("x", [P, ST, D])
        h_hi = sb("h_hi", [P, KT, S], F32R)
        h_lo = sb("h_lo", [P, KT, S], F32R)
        raw = [sb(f"raw{i}", [P, UNIT]) for i in range(2)]
        w_hi = [sb(f"w_hi{i}", [P, UNIT], F32R) for i in range(2)]
        w_lo = [sb(f"w_lo{i}", [P, UNIT], F32R) for i in range(2)]
        g_pre = sb("g_pre", [P, D])
        tmp = sb("tmp", [P, 3, D])
        ident = sb("ident", [P, P])
        junk = sb("junk", [P, D], BF16)
        ssq = sb("ssq", [P, 16])
        rstd = sb("rstd", [P, 16])
        expo = sb("expo", [P, ST])
        eps = sb("eps", [P, ST])
        lam = sb("lam", [P, 8])
        subg = sb("subg", [P, 2])
        rel = sb("rel", [BUCKETS + 1, DIFF_HEADS])
        stat = [sb(f"stat{j}", [P, 33]) for j in range(GROUP)]
        with ExitStack() as one:
            cs = sb("cs", [P, 2, S], within=one)
        g_post = sb("g_post", [P, D])
        with ExitStack() as ret:
            yT = sb("yT", [P, RET_HEADS * RET_DV // P, S], within=ret)
            gated = sb("gated", [P, ST, RET_DV], within=ret)
            decay = sb("decay", [P, PACKED], within=ret)
            in_hi = sb("in_hi", [P, PACKED], F32R, ret)
            in_lo = sb("in_lo", [P, PACKED], F32R, ret)
            qk_hi = sb("qk_hi", [P, 4, S], F32R, ret)
            qk_lo = sb("qk_lo", [P, 4, S], F32R, ret)
            rv_hi = sb("rv_hi", [P, ST, RET_DV], F32R, ret)
            rv_lo = sb("rv_lo", [P, ST, RET_DV], F32R, ret)
        with ExitStack() as ffn:
            hidden = sb("hidden", [P, FT, S], within=ffn)
            sil = sb("sil", [P, 2, S], within=ffn)
            spare_hi = sb("spare_hi", [P, UNIT], F32R, ffn)
            spare_lo = sb("spare_lo", [P, UNIT], F32R, ffn)
            act_hi = [sb(f"act_hi{i}", [P, 2, S], F32R, ffn) for i in range(2)]
            act_lo = [sb(f"act_lo{i}", [P, 2, S], F32R, ffn) for i in range(2)]
        with ExitStack() as diff:
            oT = sb("oT", [P, KT, S], within=diff)
            q_hi = sb("q_hi", [P, GROUP, S], F32R, diff)
            q_lo = sb("q_lo", [P, GROUP, S], F32R, diff)
            k_hi = sb("k_hi", [P, GROUP, S], F32R, diff)
            k_lo = sb("k_lo", [P, GROUP, S], F32R, diff)
            v_hi = sb("v_hi", [P, ST, GROUP * DIFF_DV], F32R, diff)
            v_lo = sb("v_lo", [P, ST, GROUP * DIFF_DV], F32R, diff)
            o_n = [sb(f"o_n{j}", [P, ST, P], within=diff) for j in range(GROUP)]
            nbias = [sb(f"nbias{j}", [P, S], within=diff) for j in range(GROUP)]
            sb("under_spare", [P, 2 * UNIT], within=diff)
            aT_hi = sb("aT_hi", [P, PACKED], F32R, diff)
            aT_lo = sb("aT_lo", [P, PACKED], F32R, diff)
            lg0 = sb("lg0", [P, 2, PACKED], within=diff)
        lg = [lg0[:], tmp[:].rearrange("p a d -> p (a d)")[:, 0:2 * PACKED].rearrange("p (i n) -> p i n", i=2)]

        ps = ctx.enter_context(nc.psum_tensor("ps", [P, 8 * BANK], F32))

        def bank(b, n=1):
            return ps[:, b * BANK:(b + n) * BANK]

        def scores(t, i):
            at = 4 * BANK + 256 * i if t == 1 else 2 * BANK * i + OFF[t] - 256
            return ps[:, at:at + (t + 1) * P]

        turned_maps = ps[:, 4 * BANK + 256:7 * BANK]
        o_bank = (1, 3)
        oT_bank = ((5, 6), (6, 7))
        q_bank, k_bank, v_bank = (7, 0), (2, 7), (5, 6)

        raw_in = [sem(f"raw_in{i}") for i in range(2)]
        w_hi_made = sem("w_hi_made")
        w_split = sem("w_split")
        w_used = sem("w_used")
        w_pool = sem("w_pool")
        a_hi_made = sem("a_hi_made")
        a_split = sem("a_split")
        x_in = [sem(f"x_in{t}") for t in range(ST)]
        const_in = sem("const_in")
        cs_in = sem("cs_in")
        gpre_in = sem("gpre_in")
        gpost_in = sem("gpost_in")
        rel_in = sem("rel_in")
        lam_in = sem("lam_in")
        decay_in = sem("decay_in")
        nbias_in = [sem(f"nbias_in{j}") for j in range(GROUP)]
        bias_stored = sem("bias_stored")
        bias_spread = sem("bias_spread")
        out_done = sem("out_done")
        set_up = sem("set_up")
        bias_mm = sem("bias_mm")
        bias_cp = sem("bias_cp")
        lam_sum = sem("lam_sum")
        lam_exp = sem("lam_exp")
        lam_made = sem("lam_made")
        row_done = sem("row_done")
        post_ssq = sem("post_ssq")
        post_ms = sem("post_ms")
        post_rstd = sem("post_rstd")
        post_scaled = sem("post_scaled")
        x_added = sem("x_added")
        pre_ssq = sem("pre_ssq")
        pre_ms = sem("pre_ms")
        pre_rstd = sem("pre_rstd")
        pre_scaled = sem("pre_scaled")
        pre_turned = sem("pre_turned")
        h_hi_made = sem("h_hi_made")
        h_split = sem("h_split")
        rot_mul = sem("rot_mul")
        rot_made = sem("rot_made")
        qk_hi_made = sem("qk_hi_made")
        qk_split = sem("qk_split")
        inner_mm = sem("inner_mm")
        inner_made = sem("inner_made")
        inner_hi_made = sem("inner_hi_made")
        inner_split = sem("inner_split")
        rv_row = sem("rv_row")
        rv_hi_made = sem("rv_hi_made")
        rv_split = sem("rv_split")
        ret_mm = sem("ret_mm")
        ret_ssq = sem("ret_ssq")
        ret_ms = sem("ret_ms")
        ret_rstd = sem("ret_rstd")
        gate_row = sem("gate_row")
        gate_made = sem("gate_made")
        y_made = sem("y_made")
        y_turned = sem("y_turned")
        yT_made = sem("yT_made")
        q_tile = sem("q_tile")
        k_tile = sem("k_tile")
        v_half = sem("v_half")
        q_hi_made = sem("q_hi_made")
        q_split = sem("q_split")
        k_hi_made = sem("k_hi_made")
        k_split = sem("k_split")
        v_hi_made = sem("v_hi_made")
        v_split = sem("v_split")
        qk_mm = sem("qk_mm")
        shared_bank = sem("shared_bank")
        inputs_seen = sem("inputs_seen")
        lg_made = sem("lg_made")
        exp_made = sem("exp_made")
        recip_made = sem("recip_made")
        lam_scaled = sem("lam_scaled")
        e1_scaled = sem("e1_scaled")
        attn_made = sem("attn_made")
        a_turned = sem("a_turned")
        aT_hi_made = sem("aT_hi_made")
        aT_split = sem("aT_split")
        o_mm = sem("o_mm")
        o_sq = sem("o_sq")
        o_ssq = sem("o_ssq")
        o_ms = sem("o_ms")
        o_rstd = sem("o_rstd")
        o_normed = sem("o_normed")
        o_turned = sem("o_turned")
        oT_made = sem("oT_made")
        sil_made = sem("sil_made")
        hid_made = sem("hid_made")

        ret_in_w = A["ret_w_in"][0].rearrange("(k p) n -> p k n", p=P)
        diff_in_w = A["diff_w_in"][0].rearrange("(k p) n -> p k n", p=P)
        gate_w = [A["ffn_w_gate"][l].rearrange("(k p) n -> p k n", p=P) for l in range(2)]
        up_w = [A["ffn_w_up"][l].rearrange("(k p) n -> p k n", p=P) for l in range(2)]
        close_w = [w.rearrange("(k p) n -> p k n", p=P) for w in (
            A["ret_w_out"][0], A["ffn_w_down"][0], A["diff_w_out"][0], A["ffn_w_down"][1])]

        def turned_rows(c, t):
            b = 2 * (t % 2) if c == 0 else 2 * t
            return bank(b, 2).rearrange("p (k s) -> p k s", k=KT)

        def v_rows(t):
            return bank(v_bank[t // 2])[:, 256 * (t % 2):256 * (t % 2) + 256]

        def two_rows(half):
            return bank(v_bank[half]).rearrange("p (t n) -> p t n", t=2)

        def spread(src, n):
            return bass.AP(tensor=src.tensor, offset=src.offset, ap=[[0, P], [1, n]])

        def closing_steps(c, step, eng):
            n = CLOSERS[c][1]
            pairs = (n - 3) // 2
            step(0, 0)
            if pairs:
                with eng.Fori(0, pairs) as i:
                    for j in (1, 2):
                        step(2 * i + j, j)
            for i in range(1 + 2 * pairs, n - 1):
                step(i, i)

        block = ctx.enter_context(nc.Block())

        @block.sync
        def _(sp):
            def load(u, slot, src, free=True):
                if free:
                    sp.wait_ge(w_split, u - 1 + PRIME)
                k, n = src.shape[1], src.shape[2]
                dst = raw[slot][:, 0:k * n].rearrange("p (k n) -> p k n", k=k)
                sp.dma_start(dst, src).then_inc(raw_in[slot], 16)

            def decay_of(h):
                sp.dma_start(decay[:], A["decay"][:, bass.ds(h * PACKED, PACKED)]).then_inc(decay_in, 16)

            def ret_columns(first, h, n, j=None):
                tiles = slice(0, KT) if j is None else slice(4 * j, 4 * j + 4)
                return ret_in_w[:, tiles, bass.ds(h * n + first, n)]

            def ret_units(h):
                u = 1 + RET_N * h
                load(u, 1, ret_columns(0, h, RET_DK))
                load(u + 1, 0, ret_columns(D, h, RET_DK))
                load(u + 2, 1, ret_columns(2 * D, h, RET_DV, 1))
                load(u + 3, 0, ret_columns(4 * D, h, RET_DV, 0))
                load(u + 4, 1, ret_columns(4 * D, h, RET_DV, 1))

            for t in range(ST):
                sp.dma_start(x[:, t, :], A["x"][0, t * P:(t + 1) * P, :]).then_inc(x_in[t], 16)
                if t == 0:
                    sp.dma_start(g_pre[:], spread(A["norm_gains"][0][0], D)).then_inc(gpre_in, 16)
                    sp.dma_start(ident[:], A["ident"]).then_inc(const_in, 16)
                if t == 1:
                    load(0, 0, ret_columns(2 * D, 0, RET_DV, 0), free=False)
            sp.dma_start(cs[:], A["cos_sin"]).then_inc(cs_in, 16)
            decay_of(0)
            sp.wait_ge(w_split, PRIME)
            with sp.Fori(0, RET_HEADS - 1) as h:
                ret_units(h)
                load(6 * h + 6, 0, ret_columns(2 * D, h + 1, RET_DV, 0))
                sp.wait_ge(inner_made, h + 1)
                decay_of(h + 1)
            ret_units(RET_HEADS - 1)

            def closing(c):
                u0, n = CLOSERS[c]

                def step(i, par):
                    load(u0 + i, (u0 + par) % 2, close_w[c][:, bass.ds(2 * i, 2), :])

                load(u0, u0 % 2, close_w[c][:, 0:2, :])
                gain = A["norm_gains"][c // 2]
                sp.wait_ge(pre_scaled, ST * (c + 1))
                if c:
                    sp.wait_ge(post_scaled, ST * c)
                else:
                    sp.wait_ge(qk_split, 2 * RET_HEADS)
                sp.dma_start(g_post[:], spread(gain[2 * (c % 2) + 1], D)).then_inc(gpost_in, 16)
                if c < 3:
                    nxt = A["norm_gains"][(c + 1) // 2][2 * ((c + 1) % 2)]
                    sp.dma_start(g_pre[:], spread(nxt, D)).then_inc(gpre_in, 16)

                def but_first(i, par):
                    if not (isinstance(i, int) and i == 0):
                        step(i, par)

                closing_steps(c, but_first, sp)
                step(n - 1, n - 1)

            def gate_up(l):
                with sp.Fori(0, FFN_N) as i:
                    u = GU_U[l] + 2 * i
                    load(u, GU_U[l] % 2, gate_w[l][:, :, bass.ds(i * 256, 256)])
                    load(u + 1, (GU_U[l] + 1) % 2, up_w[l][:, :, bass.ds(i * 256, 256)])

            s0, s1 = DIFF_U % 2, (DIFF_U + 1) % 2

            def load_qk(u, g):
                load(u, s0, diff_in_w[:, :, bass.ds(g * 256, 256)])
                load(u + 1, s1, diff_in_w[:, :, bass.ds(g * 256 + D, 256)])

            def load_v(u, g):
                for j in range(2):
                    load(u + j, (s0, s1)[j], diff_in_w[:, 4 * j:4 * j + 4, bass.ds(g * 256 + 2 * D, 256)])

            def bias_tile(head, j):
                src = bias_tiles[bass.ds(head, 1)].rearrange("a p s -> (a p) s")
                sp.dma_start(nbias[j][:], src).then_inc(nbias_in[j], 16)

            closing(0)
            gate_up(0)
            closing(1)
            sp.wait_ge(hid_made, 1 + FFN_N)
            sp.wait_ge(bias_spread, 16)
            for j in range(GROUP):
                bias_tile(j, j)
            load_qk(DIFF_U, 0)
            with sp.Fori(0, GROUPS - 1) as g:
                u = DIFF_U + 2 + DIFF_N * g
                load_v(u, g)
                load_qk(u + 2, g + 1)
                for j in range(GROUP):
                    sp.wait_ge(lg_made, 16 * g + 8 * j + 8)
                    bias_tile(2 * g + 2 + j, j)
            load_v(DIFFO_U - 2, GROUPS - 1)
            closing(2)
            gate_up(1)
            closing(3)
            for t in range(ST):
                sp.wait_ge(x_added, 3 * ST + t + 1)
                sp.dma_start(out[0, t * P:(t + 1) * P, :], x[:, t, :]).then_inc(out_done, 16)
            sp.wait_ge(out_done, 16 * ST)

        @block.gpsimd
        def _(pool):
            nc.gpsimd.memset(expo[:], -0.5).then_inc(set_up, 1)
            nc.gpsimd.memset(eps[:], EPS).then_inc(set_up, 1)
            pool.wait_ge(set_up, 3)

            def rsqrt(mean_sq, ms_sem, ms_n, out_ap, done, cols):
                nc.gpsimd.tensor_tensor(out_ap, mean_sq, eps[:, 0:cols], ALU.add).then_inc(ms_sem, 1)
                pool.wait_ge(ms_sem, ms_n)
                nc.gpsimd.tensor_tensor(out_ap, out_ap, expo[:, 0:cols], ALU.pow).then_inc(done, 1)

            def pre(c, t):
                pool.wait_ge(pre_ssq, ST * c + t + 1)
                rsqrt(ssq[:, 4 + t:5 + t], pre_ms, ST * c + t + 1, rstd[:, 4 + t:5 + t], pre_rstd, 1)

            def post(c, t):
                pool.wait_ge(post_ssq, ST * c + t + 1)
                rsqrt(ssq[:, t:t + 1], post_ms, ST * c + t + 1, rstd[:, t:t + 1], post_rstd, 1)

            def boundary(c):
                post(c, 0)
                pool.wait_ge(post_scaled, ST * c + 1)
                nc.gpsimd.tensor_tensor(x[:, 0, :], x[:, 0, :], tmp[:, 0, :], ALU.add).then_inc(x_added, 1)
                post(c, 1)
                if c == 3:
                    post(c, 2)
                    post(c, 3)
                    return
                pre(c + 1, 0)
                pre(c + 1, 1)
                post(c, 2)
                post(c, 3)
                u = CLOSERS[c][0] + CLOSERS[c][1] + 1
                pool.wait_ge(w_hi_made, u + 1)
                nc.gpsimd.tensor_tensor(w_lo[u % 2][:, 0:HALF], raw[u % 2][:, 0:HALF], w_hi[u % 2][:, 0:HALF].bitcast(F32),
                                        ALU.subtract).then_inc(w_pool, 1)
                pre(c + 1, 2)
                pre(c + 1, 3)

            for t in range(ST):
                pre(0, t)
            with pool.Fori(0, RET_HEADS) as h:
                pool.wait_ge(ret_ssq, ST * h + ST)
                rsqrt(ssq[:, 8:12], ret_ms, h + 1, rstd[:, 8:12], ret_rstd, ST)
            boundary(0)
            boundary(1)

            def scale_second(head, j):
                pool.wait_ge(lam_scaled, head + 1)
                for t in range(ST):
                    e1 = lg[j][:, 1, OFF[t]:OFF[t] + (t + 1) * P]
                    nc.gpsimd.tensor_tensor(e1, e1, stat[j][:, 20 + t:21 + t].to_broadcast([P, (t + 1) * P]),
                                            ALU.mult).then_inc(e1_scaled, 1)

            def o_norm(head, j):
                pool.wait_ge(o_ssq, head + 1)
                rsqrt(stat[j][:, 24:28], o_ms, head + 1, stat[j][:, 28:32], o_rstd, ST)

            with pool.Fori(0, GROUPS) as g:
                for j in range(GROUP):
                    scale_second(2 * g + j, j)
                for j in range(GROUP):
                    o_norm(2 * g + j, j)
            boundary(2)
            boundary(3)

        @block.scalar
        def _(act):
            act.dma_start(rel[0:BUCKETS, :], A["rel_bias_table"]).then_inc(rel_in, 16)
            act.dma_start(tmp[0:BUCKETS + 1, 0, 0:640], A["buckets"]).then_inc(rel_in, 16)
            lam_tile = tmp[:, 1, 640:640 + 4 * DIFF_DH]
            act.dma_start(lam_tile, spread(A["diff_lambda"][0][0], 4 * DIFF_DH)).then_inc(lam_in, 16)
            act.dma_start(subg[:, 0:1], A["diff_subln"].rearrange("a (d b) -> (a d) b", b=1)).then_inc(lam_in, 16)

            def prep(u, slot, high=None, used=None, size=UNIT):
                act.wait_ge(w_used, (u - 1 if used is None else used) + PRIME)
                act.wait_ge(raw_in[slot], 8 * (u - slot) + 16)
                high = w_hi[slot][:] if high is None else high
                nc.scalar.activation(high, raw[slot][:, 0:size], ACT.Copy).then_inc(w_hi_made, 1)

            def mean_square(src, col, done, before):
                for s, count in before:
                    if isinstance(count, int) and count == 0:
                        continue
                    act.wait_ge(s, count)
                n = src.shape[-1]
                nc.scalar.activation(junk[:, 0:n], src, ACT.Square, scale=n ** -0.5, accum_out=ssq[:, col:col + 1]).then_inc(done, 1)

            def pre_square(c, t):
                if c == 0:
                    act.wait_ge(x_in[t], 16)
                else:
                    act.wait_ge(x_added, ST * (c - 1) + t + 1)
                before = [(pre_ssq, ST * c + t)]
                if c:
                    before.append((post_ssq, ST * (c - 1) + (2, 2, 4, 4)[t]))
                mean_square(x[:, t, :], 4 + t, pre_ssq, before)

            def pre_high(c, t):
                act.wait_ge(pre_turned, ST * c + t + 1)
                nc.scalar.activation(h_hi[:, :, t * P:(t + 1) * P],
                                     turned_rows(c, t), ACT.Copy).then_inc(h_hi_made, 1)

            def post_square(c, t):
                if t < ST - 1:
                    act.wait_ge(row_done, (ST - 1) * c + t + 1)
                else:
                    act.wait_ge(w_used, CLOSERS[c][0] + CLOSERS[c][1] + PRIME)
                mean_square(bank(2 * t, 2), t, post_ssq,
                            [(post_ssq, ST * c + t), (pre_ssq, ST * (c + 1) + (min(t, 2) if t > 1 and c < 3 else 0))])

            def boundary(c):
                nxt = CLOSERS[c][0] + CLOSERS[c][1]
                post_square(c, 0)
                if c == 3:
                    for t in range(1, ST):
                        post_square(c, t)
                    return
                prep(nxt, nxt % 2, spare_hi[:], used=nxt - 2)
                post_square(c, 1)
                pre_square(c + 1, 0)
                pre_square(c + 1, 1)
                post_square(c, 2)
                pre_high(c + 1, 0)
                pre_high(c + 1, 1)
                post_square(c, 3)
                prep(nxt + 1, (nxt + 1) % 2)
                pre_square(c + 1, 2)
                pre_square(c + 1, 3)
                pre_high(c + 1, 2)
                pre_high(c + 1, 3)

            def a_high(c, i, slot):
                src = (yT, hidden, oT, hidden)[c]
                nc.scalar.activation(act_hi[slot][:], src[:, bass.ds(2 * i, 2), :], ACT.Copy).then_inc(a_hi_made, 1)

            def closing(c):
                u0 = CLOSERS[c][0]

                def step(i, par):
                    prep(u0 + i + 1, (u0 + par + 1) % 2)
                    a_high(c, i + 1, (u0 + par + 1) % 2)

                closing_steps(c, step, act)
                boundary(c)

            def gate_up(l):
                def step(i, first=False, last=False):
                    u = GU_U[l] + 2 * i
                    if first:
                        prep(u + 2, u % 2, used=u)
                    else:
                        prep(u + 1, (GU_U[l] + 1) % 2)
                    act.wait_ge(w_used, u + 1 + PRIME)
                    act.wait_ge(hid_made, 1 + FFN_N * l + i)
                    nc.scalar.activation(sil[:], bank(0, 2).rearrange("p (a s) -> p a s", a=2), ACT.Silu)\
                        .then_inc(sil_made, 1)
                    if not first:
                        prep(u + 2, GU_U[l] % 2)
                    if last:
                        a_high(2 * l + 1, 0, (u + 2) % 2)

                step(0, first=True)
                with act.Fori(1, FFN_N - 1) as i:
                    step(i)
                step(FFN_N - 1, last=True)

            pre_square(0, 0)
            pre_square(0, 1)
            pre_high(0, 0)
            prep(0, 0)
            pre_square(0, 2)
            pre_high(0, 1)
            pre_square(0, 3)
            pre_high(0, 2)
            pre_high(0, 3)
            prep(1, 1, used=0)
            act.wait_ge(lam_sum, 2)
            nc.scalar.activation(lam[:, 2:4], lam[:, 0:2], ACT.Exp).then_inc(lam_exp, 1)
            act.wait_ge(bias_cp, 1)
            act.dma_start(bias_rows, tmp[0:DIFF_HEADS, 1, 0:640]).then_inc(bias_stored, 16)
            act.wait_ge(bias_stored, 16)
            diagonals = bass.AP(tensor=bias_rows.tensor, offset=bias_rows.offset + P - 1, ap=[[640, DIFF_HEADS], [-1, P], [1, S]])
            act.dma_start(bias_tiles, diagonals).then_inc(bias_spread, 16)

            def ret_head(h, last=False):
                u = 1 + RET_N * h
                for j in range(2):
                    prep(u + 1 + j, j)
                    act.wait_ge(rot_made, 2 * h + 1 + j)
                    nc.scalar.activation(qk_hi[:, 2 * j:2 * j + 2, :], tmp[:, 0, :].rearrange("p (a s) -> p a s", a=2),
                                         ACT.Copy).then_inc(qk_hi_made, 1)
                prep(u + 3, 0)
                for t in range(ST):
                    if t < ST - 1:
                        act.wait_ge(rv_row, (ST - 1) * h + t + 1)
                    else:
                        act.wait_ge(w_used, u + 3 + PRIME)
                    nc.scalar.activation(rv_hi[:, t, :], bank(4 + t), ACT.Copy).then_inc(rv_hi_made, 1)
                prep(u + 4, 1)
                act.wait_ge(inner_made, h + 1)
                nc.scalar.activation(in_hi[:], tmp[:].rearrange("p a d -> p (a d)")[:, 0:PACKED],
                                     ACT.Copy).then_inc(inner_hi_made, 1)
                prep(u + 5, 0)
                for t in range(ST):
                    act.wait_ge(ret_mm, ST * h + t + 1)
                    mean_square(bank(t), 8 + t, ret_ssq, [(ret_ssq, ST * h + t)] if t else [])
                if last:
                    a_high(0, 0, RETO_U % 2)
                for t in range(ST):
                    if t < ST - 1:
                        act.wait_ge(gate_row, (ST - 1) * h + t + 1)
                    else:
                        act.wait_ge(w_used, u + 5 + PRIME)
                    nc.scalar.activation(gated[:, t, :], bank(4 + t), ACT.Silu).then_inc(gate_made, 1)
                if not last:
                    prep(u + 6, 1)
                for t in range(ST):
                    act.wait_ge(y_turned, ST * h + t + 1)
                    nc.scalar.activation(yT[:, bass.ds(4 * h, 4), t * P:(t + 1) * P],
                                         bank(t).rearrange("p (a s) -> p a s", a=4), ACT.Copy).then_inc(yT_made, 1)

            with act.Fori(0, RET_HEADS - 1) as h:
                ret_head(h)
            ret_head(RET_HEADS - 1, last=True)
            closing(0)
            gate_up(0)
            closing(1)

            def q_high(j, b):
                nc.scalar.activation(q_hi[:, j, :], bank(b), ACT.Copy, scale=-(DIFF_DH ** -0.5)).then_inc(q_hi_made, 1)

            def k_high(j, b):
                nc.scalar.activation(k_hi[:, j, :], bank(b), ACT.Copy).then_inc(k_hi_made, 1)

            def v_high(half):
                nc.scalar.activation(v_hi[:, 2 * half:2 * half + 2, :], two_rows(half), ACT.Copy).then_inc(v_hi_made, 1)

            def exps(head, j):
                for n, (t, i) in enumerate(ORDER):
                    act.wait_ge(lg_made, 8 * head + n + 1)
                    e = lg[j][:, i, OFF[t]:OFF[t] + (t + 1) * P]
                    nc.scalar.activation(e, e, ACT.Exp, bias=stat[j][:, 4 * i + t:4 * i + t + 1], scale=-1.0,
                                         accum_out=stat[j][:, 8 + 4 * i + t:9 + 4 * i + t]).then_inc(exp_made, 1)

            def aT_high(head):
                act.wait_ge(a_turned, head + 1)
                nc.scalar.activation(aT_hi[:], turned_maps, ACT.Copy).then_inc(aT_hi_made, 1)

            def o_square(head, j):
                act.wait_ge(o_mm, head + 1)
                nc.scalar.activation(o_n[j][:], bank(o_bank[j]).rearrange("p (a d) -> p a d", a=ST),
                                     ACT.Square, scale=DIFF_DV ** -0.5).then_inc(o_sq, 1)

            def oT_copy(head, j, b):
                act.wait_ge(o_turned, head + 1)
                nc.scalar.activation(oT[:, bass.ds(head, 1), :].rearrange("p a s -> p (a s)"), bank(b), ACT.Copy,
                                     scale=subg[:, 1:2]).then_inc(oT_made, 1)

            s0, s1 = DIFF_U % 2, (DIFF_U + 1) % 2

            def prep_v(u, used):
                prep(u, s0, spare_hi[:, 0:HALF], used, HALF)
                prep(u + 1, s1, spare_hi[:, HALF:UNIT], used, HALF)

            act.wait_ge(w_used, DIFF_U + 1 + PRIME)
            for j in range(GROUP):
                q_high(j, j)
            prep_v(DIFF_U + 2, DIFF_U + 1)
            act.wait_ge(w_used, DIFF_U + 2 + PRIME)
            for j in range(GROUP):
                k_high(j, 2 + j)

            with act.Fori(0, GROUPS - 1) as g:
                u = DIFF_U + 2 + DIFF_N * g
                head = 2 * g
                prep(u + 2, s0, used=u)
                exps(head, 0)
                prep(u + 3, s1, used=u)
                act.wait_ge(v_half, g + 1)
                v_high(0)
                act.wait_ge(w_used, u + 2 + PRIME)
                v_high(1)
                exps(head + 1, 1)
                act.wait_ge(q_tile, g + 1)
                q_high(0, q_bank[0])
                aT_high(head)
                act.wait_ge(w_used, u + 3 + PRIME)
                q_high(1, q_bank[1])
                aT_high(head + 1)
                o_square(head, 0)
                prep_v(u + 4, u + 2)
                act.wait_ge(k_tile, g + 1)
                k_high(0, k_bank[0])
                o_square(head + 1, 1)
                act.wait_ge(w_used, u + 4 + PRIME)
                k_high(1, k_bank[1])
                for j in range(GROUP):
                    oT_copy(head + j, j, oT_bank[0][j])
            g, head, u = GROUPS - 1, DIFF_HEADS - GROUP, DIFFO_U - 2
            prep(DIFFO_U, s0, used=u)
            exps(head, 0)
            act.wait_ge(v_half, g + 1)
            v_high(0)
            act.wait_ge(w_used, u + 2 + PRIME)
            v_high(1)
            exps(head + 1, 1)
            aT_high(head)
            o_square(head, 0)
            aT_high(head + 1)
            o_square(head + 1, 1)
            a_high(2, 0, DIFFO_U % 2)
            for j in range(GROUP):
                oT_copy(head + j, j, oT_bank[1][j])
            closing(2)
            gate_up(1)
            closing(3)

        @block.vector
        def _(dve):
            nc.vector.memset(rel[BUCKETS:BUCKETS + 1, :], MASKED).then_inc(set_up, 1)
            dve.sem_inc(w_split, PRIME)
            dve.sem_inc(w_used, PRIME)
            dve.sem_inc(hid_made, 1)
            dve.sem_inc(yT_made, ST)
            dve.sem_inc(oT_made, 1)

            def low(out_ap, whole, high, done):
                nc.vector.tensor_tensor(out_ap, whole, high.bitcast(F32), ALU.subtract).then_inc(done, 1)

            def prep(u, slot, low_ap=None, high=None, size=UNIT):
                dve.wait_ge(w_hi_made, u + 1)
                low_ap, high = (w_lo[slot][:], w_hi[slot][:]) if low_ap is None else (low_ap, high)
                low(low_ap, raw[slot][:, 0:size], high, w_split)

            def pre_scale(c, t):
                dve.wait_ge(pre_rstd, ST * c + t + 1)
                if t == 0:
                    dve.wait_ge(gpre_in, 16 * (c + 1))
                if t >= 1:
                    dve.wait_ge(pre_turned, ST * c + t)
                nc.vector.scalar_tensor_tensor(out=tmp[:, 2, :], in0=x[:, t, :], scalar=rstd[:, 4 + t:5 + t],
                                               in1=g_pre[:], op0=ALU.mult, op1=ALU.mult).then_inc(pre_scaled, 1)

            def pre_low(c, t):
                dve.wait_ge(h_hi_made, ST * c + t + 1)
                low(h_lo[:, :, t * P:(t + 1) * P], turned_rows(c, t),
                    h_hi[:, :, t * P:(t + 1) * P], h_split)

            def post_scale(c, t):
                dve.wait_ge(post_rstd, ST * c + t + 1)
                if t == 0:
                    dve.wait_ge(gpost_in, 16 * (c + 1))
                if t >= 2:
                    dve.wait_ge(x_added, ST * c + t - 1)
                nc.vector.scalar_tensor_tensor(out=tmp[:, t % 2, :], in0=bank(2 * t, 2),
                                               scalar=rstd[:, t:t + 1], in1=g_post[:],
                                               op0=ALU.mult, op1=ALU.mult).then_inc(post_scaled, 1)

            def post_add(c, t):
                dve.wait_ge(post_scaled, ST * c + t + 1)
                dve.wait_ge(x_added, ST * c + t)
                nc.vector.tensor_tensor(x[:, t, :], x[:, t, :], tmp[:, t % 2, :], ALU.add).then_inc(x_added, 1)

            def boundary(c):
                post_scale(c, 0)
                if c == 3:
                    for t in range(1, ST):
                        post_scale(c, t)
                        post_add(c, t)
                    return
                nxt = CLOSERS[c][0] + CLOSERS[c][1]
                prep(nxt, nxt % 2, spare_lo[:], spare_hi[:])
                post_scale(c, 1)
                post_add(c, 1)
                pre_scale(c + 1, 0)
                pre_scale(c + 1, 1)
                post_scale(c, 2)
                pre_low(c + 1, 0)
                post_add(c, 2)
                pre_low(c + 1, 1)
                post_scale(c, 3)
                post_add(c, 3)
                dve.wait_ge(w_hi_made, nxt + 2)
                dve.wait_ge(w_pool, c + 1)
                s = (nxt + 1) % 2
                low(w_lo[s][:, HALF:UNIT], raw[s][:, HALF:UNIT], w_hi[s][:, HALF:UNIT], w_split)
                pre_scale(c + 1, 2)
                pre_scale(c + 1, 3)
                pre_low(c + 1, 2)
                pre_low(c + 1, 3)

            def a_low(c, i, slot):
                src = (yT, hidden, oT, hidden)[c]
                dve.wait_ge(a_hi_made, CLOSER_BASE[c] + i + 1)
                low(act_lo[slot][:], src[:, bass.ds(2 * i, 2), :], act_hi[slot][:], a_split)

            def closing(c):
                u0 = CLOSERS[c][0]

                def step(i, par):
                    prep(u0 + i + 1, (u0 + par + 1) % 2)
                    a_low(c, i + 1, (u0 + par + 1) % 2)

                closing_steps(c, step, dve)
                boundary(c)

            def gate_up(l):
                def step(i, first=False, last=False):
                    u = GU_U[l] + 2 * i
                    if not first:
                        prep(u + 1, (GU_U[l] + 1) % 2)
                    prep(u + 2, GU_U[l] % 2)
                    if last:
                        a_low(2 * l + 1, 0, (u + 2) % 2)
                    dve.wait_ge(sil_made, FFN_N * l + i + 1)
                    dve.wait_ge(w_used, u + 2 + PRIME)
                    nc.vector.tensor_tensor(hidden[:, bass.ds(2 * i, 2), :], sil[:],
                                            bank(2, 2).rearrange("p (a s) -> p a s", a=2), ALU.mult)\
                        .then_inc(hid_made, 1)

                step(0, first=True)
                with dve.Fori(1, FFN_N - 1) as i:
                    step(i)
                step(FFN_N - 1, last=True)

            pre_scale(0, 0)
            pre_scale(0, 1)
            pre_low(0, 0)
            prep(0, 0)
            pre_scale(0, 2)
            pre_low(0, 1)
            pre_scale(0, 3)
            pre_low(0, 2)
            dve.wait_ge(bias_mm, 1)
            nc.vector.tensor_copy(tmp[0:DIFF_HEADS, 1, 0:640], ps[0:DIFF_HEADS, 6 * BANK:6 * BANK + 640]).then_inc(bias_cp, 1)
            pre_low(0, 3)
            prep(1, 1)
            dve.wait_ge(lam_in, 32)
            lt = tmp[:, 1, 640:640 + 4 * DIFF_DH]
            for i in range(2):
                a, b = lt[:, 128 * i:128 * i + 64], lt[:, 128 * i + 64:128 * i + 128]
                nc.vector.tensor_tensor_reduce(out=junk[:, 64 * i:64 * i + 64],
                                               in0=a, in1=b, scale=1.0, scalar=0.0,
                                               op0=ALU.mult, op1=ALU.add, accum_out=lam[:, i:i + 1]).then_inc(lam_sum, 1)
            dve.wait_ge(lam_exp, 1)
            nc.vector.tensor_tensor(lam[:, 4:5], lam[:, 3:4], lam[:, 2:3], ALU.subtract).then_inc(lam_made, 1)
            nc.vector.tensor_scalar(subg[:, 1:2], subg[:, 0:1], 1.0 - LAMBDA_INIT, None, ALU.mult).then_inc(lam_made, 1)
            dve.wait_ge(lam_made, 2)
            nc.vector.tensor_scalar(lam[:, 5:6], lam[:, 4:5], -LAMBDA_INIT, None, ALU.add).then_inc(lam_made, 1)
            dve.wait_ge(bias_stored, 16)
            dve.wait_ge(cs_in, 16)

            def ret_head(h, last=False):
                u = 1 + RET_N * h
                ac = tmp[:, 0, :].rearrange("p (a s) -> p a s", a=2)
                bd = tmp[:, 1, :].rearrange("p (a s) -> p a s", a=2)
                for j in range(2):
                    prep(u + 1 + j, j)
                    dve.wait_ge(w_used, u + 1 + j + PRIME)
                    if j:
                        dve.wait_ge(qk_split, 2 * h + 1)
                    x1, x2 = bank(2 * j), bank(2 * j + 1)
                    nc.vector.tensor_tensor(ac[:, 0, :], x1, cs[:, 0, :], ALU.mult)
                    nc.vector.tensor_tensor(bd[:, 0, :], x2, cs[:, 1, :], ALU.mult)
                    nc.vector.tensor_tensor(ac[:, 1, :], x1, cs[:, 1, :], ALU.mult)
                    nc.vector.tensor_tensor(bd[:, 1, :], x2, cs[:, 0, :], ALU.mult).then_inc(rot_mul, 1)
                    dve.wait_ge(rot_mul, 2 * h + 1 + j)
                    nc.vector.tensor_tensor(ac[:, 0, :], ac[:, 0, :], bd[:, 0, :], ALU.subtract)
                    nc.vector.tensor_tensor(ac[:, 1, :], ac[:, 1, :], bd[:, 1, :], ALU.add).then_inc(rot_made, 1)
                    dve.wait_ge(qk_hi_made, 2 * h + 1 + j)
                    low(qk_lo[:, 2 * j:2 * j + 2, :], ac, qk_hi[:, 2 * j:2 * j + 2, :], qk_split)
                prep(u + 3, 0)
                for t in range(ST):
                    dve.wait_ge(rv_hi_made, ST * h + t + 1)
                    low(rv_lo[:, t, :], bank(4 + t), rv_hi[:, t, :], rv_split)
                prep(u + 4, 1)
                dve.wait_ge(inner_mm, h + 1)
                dve.wait_ge(decay_in, 16 * h + 16)
                inner = tmp[:].rearrange("p a d -> p (a d)")[:, 0:PACKED]
                nc.vector.tensor_tensor(inner, ps[:, 0:PACKED], decay[:], ALU.mult).then_inc(inner_made, 1)
                dve.wait_ge(inner_hi_made, h + 1)
                low(in_lo[:], inner, in_hi[:], inner_split)
                prep(u + 5, 0)
                if last:
                    a_low(0, 0, RETO_U % 2)
                dve.wait_ge(ret_rstd, h + 1)
                for t in range(ST):
                    dve.wait_ge(gate_made, ST * h + t + 1)
                    nc.vector.scalar_tensor_tensor(out=gated[:, t, :], in0=bank(t), scalar=rstd[:, 8 + t:9 + t],
                                                   in1=gated[:, t, :], op0=ALU.mult, op1=ALU.mult).then_inc(y_made, 1)
                if not last:
                    prep(u + 6, 1)

            with dve.Fori(0, RET_HEADS - 1) as h:
                ret_head(h)
            ret_head(RET_HEADS - 1, last=True)
            closing(0)
            gate_up(0)
            closing(1)

            def q_low(head, j, b):
                dve.wait_ge(q_hi_made, head + 1)
                nc.vector.scalar_tensor_tensor(out=q_lo[:, j, :], in0=bank(b), scalar=-(DIFF_DH ** -0.5),
                                               in1=q_hi[:, j, :].bitcast(F32), op0=ALU.mult,
                                               op1=ALU.subtract).then_inc(q_split, 1)

            def k_low(head, j, b):
                dve.wait_ge(k_hi_made, head + 1)
                low(k_lo[:, j, :], bank(b), k_hi[:, j, :], k_split)

            def v_low(g, half):
                dve.wait_ge(v_hi_made, 2 * g + half + 1)
                at = slice(2 * half, 2 * half + 2)
                low(v_lo[:, at, :], two_rows(half), v_hi[:, at, :], v_split)

            def logits(head, j):
                dve.wait_ge(qk_mm, head + 1)
                dve.wait_ge(nbias_in[j], 8 * (head - j) + 16)
                nc.vector.memset(stat[j][:, 32:33], 0.0).then_inc(inputs_seen, 1)
                dve.wait_ge(lam_made, 3)
                for n, (t, i) in enumerate(ORDER):
                    w = (t + 1) * P
                    nc.vector.tensor_tensor_reduce(out=lg[j][:, i, OFF[t]:OFF[t] + w], in0=scores(t, i),
                                                   in1=nbias[j][:, S - w:S], scale=1.0, scalar=3e38,
                                                   op0=ALU.add, op1=ALU.min,
                                                   accum_out=stat[j][:, 4 * i + t:4 * i + t + 1]).then_inc(lg_made, 1)

            def over_sums(head, j):
                st = stat[j]
                dve.wait_ge(inputs_seen, head + 1)
                dve.wait_ge(exp_made, 8 * head + 8)
                nc.vector.reciprocal(st[:, 16:24], st[:, 8:16]).then_inc(recip_made, 1)
                dve.wait_ge(recip_made, head + 1)
                nc.vector.tensor_scalar(st[:, 20:24], st[:, 20:24], lam[:, 5:6], None, ALU.mult).then_inc(lam_scaled, 1)

            def attn(head, j):
                for t in range(ST):
                    dve.wait_ge(e1_scaled, ST * head + t + 1)
                    w = (t + 1) * P
                    e0, e1 = (lg[j][:, i, OFF[t]:OFF[t] + w] for i in range(2))
                    nc.vector.scalar_tensor_tensor(out=e0, in0=e0, scalar=stat[j][:, 16 + t:17 + t], in1=e1,
                                                   op0=ALU.mult, op1=ALU.add).then_inc(attn_made, 1)

            def aT_low(head):
                dve.wait_ge(aT_hi_made, head + 1)
                low(aT_lo[:], turned_maps, aT_hi[:], aT_split)

            def o_norm(head, j):
                st = stat[j]
                dve.wait_ge(o_sq, head + 1)
                nc.vector.tensor_reduce(st[:, 24:28], o_n[j][:], AX_X, ALU.add).then_inc(o_ssq, 1)
                dve.wait_ge(o_rstd, head + 1)
                nc.vector.tensor_tensor(o_n[j][:], bank(o_bank[j]).rearrange("p (a d) -> p a d", a=ST),
                                        st[:, 28:32].unsqueeze(2).to_broadcast([P, ST, P]), ALU.mult)\
                    .then_inc(o_normed, 1)

            s0, s1 = DIFF_U % 2, (DIFF_U + 1) % 2

            def prep_v(u):
                prep(u, s0, spare_lo[:, 0:HALF], spare_hi[:, 0:HALF], HALF)
                prep(u + 1, s1, spare_lo[:, HALF:UNIT], spare_hi[:, HALF:UNIT], HALF)

            for j in range(GROUP):
                q_low(j, j, j)
            prep_v(DIFF_U + 2)
            for j in range(GROUP):
                k_low(j, j, 2 + j)
            with dve.Fori(0, GROUPS - 1) as g:
                u = DIFF_U + 2 + DIFF_N * g
                head = 2 * g
                logits(head, 0)
                prep(u + 2, s0)
                over_sums(head, 0)
                prep(u + 3, s1)
                v_low(g, 0)
                attn(head, 0)
                v_low(g, 1)
                logits(head + 1, 1)
                q_low(head + 2, 0, q_bank[0])
                over_sums(head + 1, 1)
                aT_low(head)
                attn(head + 1, 1)
                q_low(head + 3, 1, q_bank[1])
                aT_low(head + 1)
                o_norm(head, 0)
                prep_v(u + 4)
                k_low(head + 2, 0, k_bank[0])
                o_norm(head + 1, 1)
                k_low(head + 3, 1, k_bank[1])
            g, head = GROUPS - 1, DIFF_HEADS - GROUP
            logits(head, 0)
            prep(DIFFO_U, s0)
            over_sums(head, 0)
            v_low(g, 0)
            attn(head, 0)
            logits(head + 1, 1)
            v_low(g, 1)
            aT_low(head)
            over_sums(head + 1, 1)
            attn(head + 1, 1)
            o_norm(head, 0)
            aT_low(head + 1)
            a_low(2, 0, DIFFO_U % 2)
            o_norm(head + 1, 1)
            closing(2)
            gate_up(1)
            closing(3)

        @block.tensor
        def _(pe):
            def three(out_ap, a_hi, a_lo, b_hi, b_lo, start, stop):
                nc.tensor.matmul(out_ap, a_hi, b_hi, start=start, stop=False)
                nc.tensor.matmul(out_ap, a_hi, b_lo, start=False, stop=False)
                return nc.tensor.matmul(out_ap, a_lo, b_hi, start=False, stop=stop)

            def column_tile(w, m, out_bank, cols=slice(0, S)):
                wh, wl = (x[:].rearrange("p (k n) -> p k n", k=KT)[:, :, m * P:(m + 1) * P] for x in w)
                for k in range(KT):
                    mm = three(bank(out_bank)[:, cols], wh[:, k, :], wl[:, k, :], h_hi[:, k, cols], h_lo[:, k, cols],
                               k == 0, k == KT - 1)
                return mm

            def slot_of(i):
                return w_hi[i], w_lo[i]

            def columns(u, slot, banks):
                pe.wait_ge(w_split, u + 1 + PRIME)
                for m in range(2):
                    mm = column_tile(slot_of(slot), m, banks[m])
                mm.then_inc(w_used, 1)

            def row_tile(w, t, tiles, out_ap, n, first):
                wh, wl = (x.rearrange("p (k n) -> p k n", k=tiles) for x in w)
                at = slice(t * P, (t + 1) * P)
                for k in range(tiles):
                    kk = first + k
                    mm = three(out_ap, h_hi[:, kk, at], h_lo[:, kk, at], wh[:, k, :], wl[:, k, :], kk == 0, kk == KT - 1)
                return mm

            def ret_rows(u, slot, half, before=None, row_sem=None):
                pe.wait_ge(w_split, u + 1 + PRIME)
                for t in range(ST):
                    if before:
                        before(t)
                    mm = row_tile((w_hi[slot][:], w_lo[slot][:]), t, 4, bank(4 + t), RET_DV, 4 * half)
                    if row_sem is not None and t < ST - 1:
                        mm.then_inc(row_sem, 1)
                mm.then_inc(w_used, 1)

            def turn_rows(c, t):
                pe.wait_ge(pre_scaled, ST * c + t + 1)
                if c == 0 and t >= 2:
                    pe.wait_ge(h_split, t - 1)
                rows = turned_rows(c, t)
                for k in range(KT):
                    mm = nc.tensor.transpose(rows[:, k, :], tmp[:, 2, k * P:(k + 1) * P], ident[:])
                mm.then_inc(pre_turned, 1)

            def closing(c, order, between=None):
                u0, n = CLOSERS[c]

                def row(i, par, t, start, stop):
                    slot = (u0 + par) % 2
                    wh, wl = (w[slot][:].rearrange("p (k n) -> p k n", k=2) for w in (w_hi, w_lo))
                    at = slice(t * P, (t + 1) * P)
                    for k in range(2):
                        for half in range(2):
                            cols = slice(half * BANK, (half + 1) * BANK)
                            mm = three(bank(2 * t + half), act_hi[slot][:, k, at], act_lo[slot][:, k, at],
                                       wh[:, k, cols], wl[:, k, cols], start and k == 0, stop and k == 1)
                    return mm

                def ready(i):
                    pe.wait_ge(w_split, u0 + i + 1 + PRIME)
                    pe.wait_ge(a_split, CLOSER_BASE[c] + i + 1)

                def step(i, par):
                    ready(i)
                    first = isinstance(i, int) and i == 0
                    for m, t in enumerate(order if first else range(ST)):
                        if first and between:
                            between(m)
                        mm = row(i, par, t, first, False)
                    mm.then_inc(w_used, 1)

                def but_two(i, par):
                    if not (isinstance(i, int) and i == n - 2):
                        step(i, par)

                closing_steps(c, but_two, pe)
                ready(n - 1)
                for t in range(ST):
                    row(n - 2, n - 2, t, False, False)
                    if t == ST - 1 and c < 3:
                        turn_rows(c + 1, 1)
                    mm = row(n - 1, n - 1, t, False, True)
                    if t < ST - 1:
                        mm.then_inc(row_done, 1)
                    if t == 2 and c < 3:
                        turn_rows(c + 1, 0)
                mm.then_inc(w_used, 2)

            def after_closing(c):
                u = CLOSERS[c][0] + CLOSERS[c][1]
                for half in range(2):
                    cols = slice(half * 256, half * 256 + 256)
                    pe.wait_ge(h_split, ST * (c + 1) + 2 * half + 2)
                    for j, w in enumerate(((spare_hi, spare_lo), slot_of((u + 1) % 2))):
                        pe.wait_ge(w_split, u + j + 1 + PRIME)
                        for m in range(2):
                            mm = column_tile(w, m, 2 * j + m, cols)
                            if half == 0 and m == 0:
                                turn_rows(c + 1, 2 + j)
                        if half:
                            mm.then_inc(w_used, 1)

            def gate_up(l):
                after_closing(2 * l)
                pe.wait_ge(sil_made, FFN_N * l + 1)
                with pe.Fori(1, FFN_N) as i:
                    u = GU_U[l] + 2 * i
                    columns(u, GU_U[l] % 2, (0, 1))
                    pe.wait_ge(hid_made, 1 + FFN_N * l + i)
                    columns(u + 1, (GU_U[l] + 1) % 2, (2, 3))
                    pe.wait_ge(sil_made, FFN_N * l + i + 1)

            pe.wait_ge(const_in, 16)
            turn_rows(0, 0)
            turn_rows(0, 1)
            pe.wait_ge(rel_in, 32)
            pe.wait_ge(set_up, 3)
            for at, n in ((0, BANK), (BANK, 640 - BANK)):
                mm = nc.tensor.matmul(ps[0:DIFF_HEADS, 6 * BANK + at:6 * BANK + at + n], rel[:],
                                      tmp[0:BUCKETS + 1, 0, at:at + n], start=True, stop=True)
            mm.then_inc(bias_mm, 1)

            def first_rows(t):
                pe.wait_ge(h_split, t + 1)
                if t == 2:
                    pe.wait_ge(bias_cp, 1)

            pe.wait_ge(w_split, 1 + PRIME)
            for t in range(ST):
                first_rows(t)
                mm = row_tile((w_hi[0][:], w_lo[0][:]), t, 4, bank(4 + t), RET_DV, 0)
                if t < 2:
                    turn_rows(0, 2 + t)
            mm.then_inc(w_used, 1)

            def turn_y(h):
                for t in range(ST):
                    pe.wait_ge(y_made, ST * h + t + 1)
                    for a in range(4):
                        mm = nc.tensor.transpose(bank(t)[:, a * P:(a + 1) * P], gated[:, t, a * P:(a + 1) * P], ident[:])
                    mm.then_inc(y_turned, 1)

            def ret_head(h, last=False):
                u = 1 + RET_N * h
                pe.wait_ge(yT_made, ST * h + ST)
                columns(u, 1, (0, 1))
                columns(u + 1, 0, (2, 3))
                ret_rows(u + 2, 1, 1, row_sem=rv_row)
                pe.wait_ge(qk_split, 2 * h + 2)
                for m in (0, 1, 3, 2):
                    n = (ST - m) * P
                    at = RET_OFF[ST - 1 - m]
                    for d in range(2):
                        ks = slice(m * P, (m + 1) * P)
                        mm = three(ps[:, at:at + n], qk_hi[:, 2 + d, ks], qk_lo[:, 2 + d, ks],
                                   qk_hi[:, d, m * P:S], qk_lo[:, d, m * P:S], d == 0, d == 1)
                mm.then_inc(inner_mm, 1)
                ret_rows(u + 3, 0, 0, before=lambda t: pe.wait_ge(rv_split, ST * h + t + 1))
                pe.wait_ge(inner_split, h + 1)
                for t in range(ST):
                    for m in range(t + 1):
                        at = RET_OFF[ST - 1 - m] + (t - m) * P
                        mm = three(bank(t), in_hi[:, at:at + P], in_lo[:, at:at + P], rv_hi[:, m, :], rv_lo[:, m, :],
                                   m == 0, m == t)
                    mm.then_inc(ret_mm, 1)
                ret_rows(u + 4, 1, 1, row_sem=gate_row)
                if not last:
                    def before(t):
                        pe.wait_ge(gate_made, ST * h + t + 1)
                        if t == ST - 1:
                            turn_y(h)

                    ret_rows(u + 5, 0, 0, before=before)

            with pe.Fori(0, RET_HEADS - 1) as h:
                ret_head(h)
            h = RET_HEADS - 1
            ret_head(h, last=True)

            def between_ret(m):
                if m < 2:
                    pe.wait_ge(gate_made, ST * h + 2 * m + 2)
                if m == 1:
                    turn_y(h)
                if m >= 2:
                    pe.wait_ge(yT_made, ST * RET_HEADS + 2 * (m - 1))

            def between_ffn(l):
                def between(m):
                    if m == 2:
                        pe.wait_ge(hid_made, 1 + FFN_N * (l + 1))
                return between

            closing(0, (2, 3, 0, 1), between_ret)
            gate_up(0)
            closing(1, (2, 3, 0, 1), between_ffn(0))

            def attention_scores(head, j):
                pe.wait_ge(q_split, head + 1)
                pe.wait_ge(k_split, head + 1)
                for t, i in ORDER:
                    d = slice(DIFF_DH * i, DIFF_DH * (i + 1))
                    if (t, i) == (1, 1):
                        pe.wait_ge(shared_bank, head + 1)
                    mm = three(scores(t, i), q_hi[d, j, t * P:(t + 1) * P], q_lo[d, j, t * P:(t + 1) * P],
                               k_hi[d, j, 0:(t + 1) * P], k_lo[d, j, 0:(t + 1) * P], True, True)
                    if (t, i) == (1, 0):
                        mm.then_inc(shared_bank, 1)
                mm.then_inc(qk_mm, 1)

            def turn_maps(head, j):
                for t in range(ST):
                    pe.wait_ge(attn_made, ST * head + t + 1)
                    for k in range(t + 1):
                        at = slice(OFF[t] + k * P, OFF[t] + (k + 1) * P)
                        mm = nc.tensor.transpose(turned_maps[:, at], lg[j][:, 0, at], ident[:])
                mm.then_inc(a_turned, 1)

            def attention_out(head, j):
                pe.wait_ge(aT_split, head + 1)
                for t in range(ST):
                    o = bank(o_bank[j])[:, t * P:(t + 1) * P]
                    for k in range(t + 1):
                        at = slice(OFF[t] + k * P, OFF[t] + (k + 1) * P)
                        dv = slice(j * DIFF_DV, (j + 1) * DIFF_DV)
                        mm = three(o, aT_hi[:, at], aT_lo[:, at], v_hi[:, k, dv], v_lo[:, k, dv], k == 0, k == t)
                mm.then_inc(o_mm, 1)

            def turn_o(head, j, b):
                pe.wait_ge(o_normed, head + 1)
                for t in range(ST):
                    mm = nc.tensor.transpose(bank(b)[:, t * P:(t + 1) * P], o_n[j][:, t, :], ident[:])
                mm.then_inc(o_turned, 1)

            def v_tiles(half):
                for t in (2 * half, 2 * half + 1):
                    mm = row_tile((spare_hi[:], spare_lo[:]), t, KT, v_rows(t), 256, 0)
                return mm

            s0, s1 = DIFF_U % 2, (DIFF_U + 1) % 2
            after_closing(1)
            pe.wait_ge(k_split, GROUP)
            with pe.Fori(0, GROUPS - 1) as g:
                u = DIFF_U + 2 + DIFF_N * g
                head = 2 * g
                attention_scores(head, 0)
                pe.wait_ge(oT_made, head + 1)
                pe.wait_ge(w_split, u + 2 + PRIME)
                v_tiles(0).then_inc(v_half, 1)
                v_tiles(1).then_inc(w_used, 2)
                pe.wait_ge(lg_made, 8 * head + 8)
                attention_scores(head + 1, 1)
                pe.wait_ge(w_split, u + 3 + PRIME)
                column_tile(slot_of(s0), 0, q_bank[0]).then_inc(q_tile, 1)
                pe.wait_ge(v_split, 2 * g + 2)
                pe.wait_ge(lg_made, 8 * head + 16)
                turn_maps(head, 0)
                column_tile(slot_of(s0), 1, q_bank[1]).then_inc(w_used, 1)
                attention_out(head, 0)
                turn_maps(head + 1, 1)
                pe.wait_ge(w_split, u + 4 + PRIME)
                column_tile(slot_of(s1), 0, k_bank[0]).then_inc(k_tile, 1)
                attention_out(head + 1, 1)
                pe.wait_ge(q_split, head + 3)
                column_tile(slot_of(s1), 1, k_bank[1]).then_inc(w_used, 1)
                for j in range(GROUP):
                    turn_o(head + j, j, oT_bank[0][j])
            g, head, u = GROUPS - 1, DIFF_HEADS - GROUP, DIFFO_U - 2
            attention_scores(head, 0)
            pe.wait_ge(oT_made, head + 1)
            pe.wait_ge(w_split, u + 2 + PRIME)
            v_tiles(0).then_inc(v_half, 1)
            pe.wait_ge(lg_made, 8 * head + 8)
            attention_scores(head + 1, 1)
            v_tiles(1).then_inc(w_used, 2)
            pe.wait_ge(v_split, 2 * g + 2)
            pe.wait_ge(lg_made, 8 * head + 16)
            turn_maps(head, 0)
            attention_out(head, 0)
            turn_maps(head + 1, 1)
            attention_out(head + 1, 1)

            def between_diff(m):
                if m == 2:
                    for j in range(GROUP):
                        turn_o(head + j, j, oT_bank[1][j])
                if m == 3:
                    pe.wait_ge(oT_made, DIFF_HEADS + 1)

            pe.wait_ge(o_normed, head + 1)
            closing(2, (0, 2, 1, 3), between_diff)
            gate_up(1)
            closing(3, (2, 3, 0, 1), between_ffn(1))


ORDER = [(1, 0), (3, 0), (3, 1), (2, 0), (2, 1), (0, 0), (0, 1), (1, 1)]


def constants():
    f32 = np.float32
    half = RET_DK // 2
    inv = f32(10000.0) ** (-np.arange(half, dtype=f32) / f32(half))
    ang = (np.arange(S, dtype=f32)[None, :] * inv[:, None]).astype(f32)
    cos_sin = np.stack([np.cos(ang), np.sin(ang)], 1).astype(f32)
    log_gamma = np.log1p(-(2.0 ** (-5.0 - np.arange(RET_HEADS))))
    decay = np.zeros((RET_HEADS, P, PACKED))
    key = np.arange(P)[:, None]
    for m in range(ST):
        n = (ST - m) * P
        d = np.arange(n)[None, :] - key
        at = RET_OFF[ST - 1 - m]
        decay[:, :, at:at + n] = np.where(d >= 0, np.exp(np.maximum(d, 0) * log_gamma[:, None, None]), 0.0)
    decay = (decay * RET_DK ** -0.5).astype(f32).transpose(1, 0, 2).reshape(P, RET_HEADS * PACKED)
    dist = np.arange(S)
    exact = BUCKETS // 2
    large = exact + (np.log(np.maximum(dist, 1).astype(f32) / f32(exact)) / f32(np.log(128 / exact))
                     * f32(BUCKETS - exact)).astype(np.int32)
    bucket = np.where(dist < exact, dist, np.minimum(large, BUCKETS - 1))
    buckets = np.zeros((BUCKETS + 1, 640), f32)
    buckets[bucket[::-1], np.arange(S)] = -1.0
    buckets[BUCKETS, S:] = 1.0
    return {"cos_sin": cos_sin, "decay": np.ascontiguousarray(decay), "buckets": buckets, "ident": np.eye(P, dtype=f32)}


NAMES = ["x", "norm_gains", "ret_w_in", "ret_w_out", "diff_w_in", "diff_w_out", "diff_lambda", "diff_subln",
         "rel_bias_table", "ffn_w_gate", "ffn_w_up", "ffn_w_down"]


def kernel(**inputs):
    import concourse.bacc as bacc
    from concourse.bass_utils import run_bass_kernel_spmd

    nc = bacc.Bacc("TRN2", target_bir_lowering=False, num_devices=1)
    arrays, args = {}, {}
    for name, a in [*((n, inputs[n]) for n in NAMES), *constants().items()]:
        a = np.ascontiguousarray(a)
        arrays[f"in_{name}"] = a
        args[name] = nc.dram_tensor(f"in_{name}", a.shape, mybir.dt.from_np(a.dtype), kind="ExternalInput").ap()
    out = nc.dram_tensor("out", (1, S, D), F32, kind="ExternalOutput").ap()
    build(nc, args, out)
    r = run_bass_kernel_spmd(nc, [arrays], core_ids=[0])
    return r.results[0]["out"]
```

```python
from contextlib import ExitStack

import concourse.bass as bass
import numpy as np
from concourse import mybir

F32 = mybir.dt.float32
F32R = mybir.dt.float32r
BF16 = mybir.dt.bfloat16
ACT = mybir.ActivationFunctionType
ALU = mybir.AluOpType
AX_X = mybir.AxisListType.X

P = 128
S = 512
D = 1024
ST = S // P
KT = D // P
EPS = 1e-6
BANK = 512

RET_HEADS = 4
RET_DK = D // RET_HEADS
RET_DV = 2 * RET_DK

DIFF_HEADS = 8
DIFF_DH = D // (2 * DIFF_HEADS)
DIFF_DV = 2 * DIFF_DH
GROUP = 2
GROUPS = DIFF_HEADS // GROUP
LAMBDA_INIT = 0.8 - 0.6 * float(np.exp(-0.3))
BUCKETS = 32
MASKED = 1e30

D_FF = -(-8 * D // (3 * 256)) * 256
FT = D_FF // P

UNIT = 2048
HALF = UNIT // 2
PACKED = S + 384 + P + 256
RET_OFF = {3: 0, 2: 512, 0: 896, 1: 1024}
OFF = {1: 0, 3: 256, 2: 768, 0: 1152}

RET_N = 6
RETO_U = RET_N * RET_HEADS
RETO_N = RET_HEADS * RET_DV // (2 * P)
FFN_N = FT // 2
GU_U = [RETO_U + RETO_N, 0]
DN_U = [GU_U[0] + 2 * FFN_N, 0]
DIFF_U = DN_U[0] + FFN_N
DIFF_N = 4
DIFFO_U = DIFF_U + DIFF_N * GROUPS
DIFFO_N = KT // 2
GU_U[1] = DIFFO_U + DIFFO_N
DN_U[1] = GU_U[1] + 2 * FFN_N
CLOSERS = [(RETO_U, RETO_N), (DN_U[0], FFN_N), (DIFFO_U, DIFFO_N), (DN_U[1], FFN_N)]
CLOSER_BASE = [sum(n for _, n in CLOSERS[:c]) for c in range(4)]

PRIME = 2


def build(nc, A, out):
    bias_rows = nc.dram_tensor("bias_rows", (DIFF_HEADS, 640), F32, kind="Internal").ap()
    bias_tiles = nc.dram_tensor("bias_tiles", (DIFF_HEADS, P, S), F32, kind="Internal").ap()

    with ExitStack() as ctx:
        def sb(name, shape, dt=F32, within=ctx):
            return within.enter_context(nc.sbuf_tensor(name, shape, dt))

        def sem(name):
            return ctx.enter_context(nc.semaphore(name))

        x = sb("x", [P, ST, D])
        h_hi = sb("h_hi", [P, KT, S], F32R)
        h_lo = sb("h_lo", [P, KT, S], F32R)
        raw = [sb(f"raw{i}", [P, UNIT]) for i in range(2)]
        w_hi = [sb(f"w_hi{i}", [P, UNIT], F32R) for i in range(2)]
        w_lo = [sb(f"w_lo{i}", [P, UNIT], F32R) for i in range(2)]
        g_pre = sb("g_pre", [P, D])
        tmp = sb("tmp", [P, 3, D])
        ident = sb("ident", [P, P])
        junk = sb("junk", [P, D], BF16)
        ssq = sb("ssq", [P, 16])
        rstd = sb("rstd", [P, 16])
        expo = sb("expo", [P, ST])
        eps = sb("eps", [P, ST])
        lam = sb("lam", [P, 8])
        subg = sb("subg", [P, 2])
        rel = sb("rel", [BUCKETS + 1, DIFF_HEADS])
        stat = [sb(f"stat{j}", [P, 33]) for j in range(GROUP)]
        with ExitStack() as one:
            cs = sb("cs", [P, 2, S], within=one)
        g_post = sb("g_post", [P, D])
        with ExitStack() as ret:
            yT = sb("yT", [P, RET_HEADS * RET_DV // P, S], within=ret)
            gated = sb("gated", [P, ST, RET_DV], within=ret)
            decay = sb("decay", [P, PACKED], within=ret)
            in_hi = sb("in_hi", [P, PACKED], F32R, ret)
            in_lo = sb("in_lo", [P, PACKED], F32R, ret)
            qk_hi = sb("qk_hi", [P, 4, S], F32R, ret)
            qk_lo = sb("qk_lo", [P, 4, S], F32R, ret)
            rv_hi = sb("rv_hi", [P, ST, RET_DV], F32R, ret)
            rv_lo = sb("rv_lo", [P, ST, RET_DV], F32R, ret)
        with ExitStack() as ffn:
            hidden = sb("hidden", [P, FT, S], within=ffn)
            sil = sb("sil", [P, 2, S], within=ffn)
            spare_hi = sb("spare_hi", [P, UNIT], F32R, ffn)
            spare_lo = sb("spare_lo", [P, UNIT], F32R, ffn)
            act_hi = [sb(f"act_hi{i}", [P, 2, S], F32R, ffn) for i in range(3)]
            act_lo = [sb(f"act_lo{i}", [P, 2, S], F32R, ffn) for i in range(3)]
        with ExitStack() as diff:
            oT = sb("oT", [P, KT, S], within=diff)
            q_hi = sb("q_hi", [P, GROUP, S], F32R, diff)
            q_lo = sb("q_lo", [P, GROUP, S], F32R, diff)
            k_hi = sb("k_hi", [P, GROUP, S], F32R, diff)
            k_lo = sb("k_lo", [P, GROUP, S], F32R, diff)
            v_parts = sb("v_parts", [P, ST, GROUP, 2, DIFF_DV], F32R, diff)
            o_n = [sb(f"o_n{j}", [P, ST, P], within=diff) for j in range(GROUP)]
            nbias = [sb(f"nbias{j}", [P, S], within=diff) for j in range(GROUP)]
            sb("under_spare", [P, 2 * UNIT], within=diff)
            aT_hi = sb("aT_hi", [P, PACKED], F32R, diff)
            aT_lo = sb("aT_lo", [P, PACKED], F32R, diff)
            lg0 = sb("lg0", [P, 2, PACKED], within=diff)
        act_parts = [*zip(act_hi, act_lo), (q_hi, q_lo), (k_hi, k_lo)]
        lg = [lg0[:], tmp[:].rearrange("p a d -> p (a d)")[:, 0:2 * PACKED].rearrange("p (i n) -> p i n", i=2)]

        ps = ctx.enter_context(nc.psum_tensor("ps", [P, 8 * BANK], F32))

        def bank(b, n=1):
            return ps[:, b * BANK:(b + n) * BANK]

        def scores(t, i):
            at = 4 * BANK + 256 * i if t == 1 else 2 * BANK * i + OFF[t] - 256
            return ps[:, at:at + (t + 1) * P]

        turned_maps = ps[:, 4 * BANK + 256:7 * BANK]
        oT_bank = (5, 6)
        last_oT_bank = (4, 6)
        o_bank = (1, 5)
        q_bank, k_bank, v_bank = (7, 0), (0, 7), (5, 6)

        raw_in = [sem(f"raw_in{i}") for i in range(2)]
        w_hi_made = sem("w_hi_made")
        w_split = sem("w_split")
        w_used = sem("w_used")
        first_in = sem("first_in")
        first_hi_made = sem("first_hi_made")
        first_split = sem("first_split")
        w_pool = sem("w_pool")
        a_hi_made = sem("a_hi_made")
        a_split = sem("a_split")
        x_in = [sem(f"x_in{t}") for t in range(ST)]
        const_in = sem("const_in")
        cs_in = sem("cs_in")
        gpre_in = sem("gpre_in")
        gpost_in = sem("gpost_in")
        rel_in = sem("rel_in")
        lam_in = sem("lam_in")
        decay_in = sem("decay_in")
        nbias_in = [sem(f"nbias_in{j}") for j in range(GROUP)]
        bias_stored = sem("bias_stored")
        bias_spread = sem("bias_spread")
        out_done = sem("out_done")
        set_up = sem("set_up")
        bias_mm = sem("bias_mm")
        bias_cp = sem("bias_cp")
        warm = sem("warm")
        lam_sum = sem("lam_sum")
        lam_exp = sem("lam_exp")
        lam_made = sem("lam_made")
        row_done = sem("row_done")
        post_ssq = sem("post_ssq")
        post_ms = sem("post_ms")
        post_rstd = sem("post_rstd")
        post_scaled = sem("post_scaled")
        x_added = sem("x_added")
        pre_ssq = sem("pre_ssq")
        pre_ms = sem("pre_ms")
        pre_rstd = sem("pre_rstd")
        pre_scaled = sem("pre_scaled")
        pre_turned = sem("pre_turned")
        h_hi_made = sem("h_hi_made")
        h_split = sem("h_split")
        rot_mul = sem("rot_mul")
        rot_made = sem("rot_made")
        qk_hi_made = sem("qk_hi_made")
        qk_split = sem("qk_split")
        inner_mm = sem("inner_mm")
        inner_made = sem("inner_made")
        inner_hi_made = sem("inner_hi_made")
        inner_split = sem("inner_split")
        rv_row = sem("rv_row")
        rv_hi_made = sem("rv_hi_made")
        rv_split = sem("rv_split")
        ret_mm = sem("ret_mm")
        ret_ssq = sem("ret_ssq")
        ret_ms = sem("ret_ms")
        ret_rstd = sem("ret_rstd")
        gate_row = sem("gate_row")
        gate_made = sem("gate_made")
        y_made = sem("y_made")
        y_turned = sem("y_turned")
        yT_made = sem("yT_made")
        q_tile = sem("q_tile")
        k_tile = sem("k_tile")
        v_half = sem("v_half")
        q_hi_made = sem("q_hi_made")
        q_split = sem("q_split")
        k_hi_made = sem("k_hi_made")
        k_split = sem("k_split")
        v_hi_made = sem("v_hi_made")
        v_split = sem("v_split")
        qk_mm = sem("qk_mm")
        shared_bank = sem("shared_bank")
        inputs_seen = sem("inputs_seen")
        lg_made = sem("lg_made")
        exp_made = sem("exp_made")
        recip_made = sem("recip_made")
        lam_scaled = sem("lam_scaled")
        e1_scaled = sem("e1_scaled")
        attn_made = sem("attn_made")
        a_turned = sem("a_turned")
        aT_hi_made = sem("aT_hi_made")
        aT_split = sem("aT_split")
        o_mm = sem("o_mm")
        o_summed = sem("o_summed")
        o_sq = sem("o_sq")
        o_ssq = sem("o_ssq")
        o_ms = sem("o_ms")
        o_rstd = sem("o_rstd")
        o_normed = sem("o_normed")
        o_turned = sem("o_turned")
        oT_made = sem("oT_made")
        sil_made = sem("sil_made")
        hid_made = sem("hid_made")

        ret_in_w = A["ret_w_in"][0].rearrange("(k p) n -> p k n", p=P)
        diff_in_w = A["diff_w_in"][0].rearrange("(k p) n -> p k n", p=P)
        gate_w = [A["ffn_w_gate"][l].rearrange("(k p) n -> p k n", p=P) for l in range(2)]
        up_w = [A["ffn_w_up"][l].rearrange("(k p) n -> p k n", p=P) for l in range(2)]
        close_w = [w.rearrange("(k p) n -> p k n", p=P) for w in (
            A["ret_w_out"][0], A["ffn_w_down"][0], A["diff_w_out"][0], A["ffn_w_down"][1])]

        def turned_rows(c, t):
            b = 2 * (t % 2) if c == 0 else 2 * t
            return bank(b, 2).rearrange("p (k s) -> p k s", k=KT)

        def v_rows(t, last=False):
            b = 7 if last and t >= 2 else v_bank[t // 2]
            return bank(b)[:, 256 * (t % 2):256 * (t % 2) + 256]

        def two_rows(half, last=False):
            return bank(7 if last and half else v_bank[half]).rearrange("p (t j n) -> p t j n", t=2, j=GROUP)

        def o_part(j, part):
            return bank(o_bank[j], 2).rearrange("p (t a d) -> p t a d", t=ST, a=2)[:, :, part, :]

        def spread(src, n):
            return bass.AP(tensor=src.tensor, offset=src.offset, ap=[[0, P], [1, n]])

        def weight_parts(slot):
            return (w_hi[slot][:], w_lo[slot][:]) if slot < 2 else (spare_hi[:], spare_lo[:])

        def last_slots(c):
            a, b = (CLOSERS[c][0] + CLOSERS[c][1] - 1) % 2, (CLOSERS[c][0] + CLOSERS[c][1]) % 2
            return (b, 2, a, b) if c == 1 else (2, b, a, 2)

        def closing_steps(c, step, eng):
            n = CLOSERS[c][1]
            pairs = (n - 4) // 2
            step(0, 0)
            if pairs:
                with eng.Fori(0, pairs) as i:
                    for j in (1, 2):
                        step(2 * i + j, j)
            for i in range(1 + 2 * pairs, n - 3):
                step(i, i)

        block = ctx.enter_context(nc.Block())

        @block.sync
        def _(sp):
            def load(u, slot, src):
                sp.wait_ge(w_split, u - 1 + PRIME)
                k, n = src.shape[1], src.shape[2]
                dst = raw[slot][:, 0:k * n].rearrange("p (k n) -> p k n", k=k)
                sp.dma_start(dst, src).then_inc(raw_in[slot], 16)

            def decay_of(h):
                sp.dma_start(decay[:], A["decay"][:, bass.ds(h * PACKED, PACKED)]).then_inc(decay_in, 16)

            def ret_columns(first, h, n, j=None):
                tiles = slice(0, KT) if j is None else slice(4 * j, 4 * j + 4)
                return ret_in_w[:, tiles, bass.ds(h * n + first, n)]

            def ret_units(h):
                u = 1 + RET_N * h
                load(u, 1, ret_columns(0, h, RET_DK))
                load(u + 1, 0, ret_columns(D, h, RET_DK))
                load(u + 2, 1, ret_columns(2 * D, h, RET_DV, 1))
                load(u + 3, 0, ret_columns(4 * D, h, RET_DV, 0))
                load(u + 4, 1, ret_columns(4 * D, h, RET_DV, 1))

            for t in range(ST):
                sp.dma_start(x[:, t, :], A["x"][0, t * P:(t + 1) * P, :]).then_inc(x_in[t], 16)
                if t == 0:
                    sp.dma_start(g_pre[:], spread(A["norm_gains"][0][0], D)).then_inc(gpre_in, 16)
                    sp.dma_start(ident[:], A["ident"]).then_inc(const_in, 16)
                if t == 1:
                    first = ret_columns(2 * D, 0, RET_DV, 0)
                    for half, done in enumerate((first_in, raw_in[0])):
                        dst = raw[0][:, half * HALF:(half + 1) * HALF].rearrange("p (k n) -> p k n", k=2)
                        sp.dma_start(dst, first[:, 2 * half:2 * half + 2, :]).then_inc(done, 16)
            sp.wait_ge(w_split, PRIME)
            with sp.Fori(0, RET_HEADS - 1) as h:
                ret_units(h)
                load(6 * h + 6, 0, ret_columns(2 * D, h + 1, RET_DV, 0))
                sp.wait_ge(inner_made, h + 1)
                decay_of(h + 1)
            ret_units(RET_HEADS - 1)

            def closing(c):
                u0, n = CLOSERS[c]

                def step(i, par):
                    load(u0 + i, (u0 + par) % 2, close_w[c][:, bass.ds(2 * i, 2), :])

                load(u0, u0 % 2, close_w[c][:, 0:2, :])
                gain = A["norm_gains"][c // 2]
                sp.wait_ge(pre_scaled, ST * (c + 1))
                if c:
                    sp.wait_ge(post_scaled, ST * c)
                else:
                    sp.wait_ge(qk_split, 2 * RET_HEADS)
                sp.dma_start(g_post[:], spread(gain[2 * (c % 2) + 1], D)).then_inc(gpost_in, 16)
                if c < 3:
                    nxt = A["norm_gains"][(c + 1) // 2][2 * ((c + 1) % 2)]
                    sp.dma_start(g_pre[:], spread(nxt, D)).then_inc(gpre_in, 16)

                def but_first(i, par):
                    if not (isinstance(i, int) and i == 0):
                        step(i, par)

                closing_steps(c, but_first, sp)
                for i in range(n - 3, n):
                    step(i, i)

            def gate_up(l):
                with sp.Fori(0, FFN_N) as i:
                    u = GU_U[l] + 2 * i
                    load(u, GU_U[l] % 2, gate_w[l][:, :, bass.ds(i * 256, 256)])
                    load(u + 1, (GU_U[l] + 1) % 2, up_w[l][:, :, bass.ds(i * 256, 256)])

            s0, s1 = DIFF_U % 2, (DIFF_U + 1) % 2

            def load_qk(u, g):
                load(u, s0, diff_in_w[:, :, bass.ds(g * 256, 256)])
                load(u + 1, s1, diff_in_w[:, :, bass.ds(g * 256 + D, 256)])

            def load_v(u, g):
                for j in range(2):
                    load(u + j, (s0, s1)[j], diff_in_w[:, 4 * j:4 * j + 4, bass.ds(g * 256 + 2 * D, 256)])

            def bias_tile(head, j):
                src = bias_tiles[bass.ds(head, 1)].rearrange("a p s -> (a p) s")
                sp.dma_start(nbias[j][:], src).then_inc(nbias_in[j], 16)

            closing(0)
            gate_up(0)
            closing(1)
            sp.wait_ge(hid_made, 1 + FFN_N)
            sp.wait_ge(bias_spread, 16)
            for j in range(GROUP):
                bias_tile(j, j)
            load_qk(DIFF_U, 0)
            with sp.Fori(0, GROUPS - 1) as g:
                u = DIFF_U + 2 + DIFF_N * g
                load_v(u, g)
                load_qk(u + 2, g + 1)
                for j in range(GROUP):
                    sp.wait_ge(lg_made, 16 * g + 8 * j + 8)
                    bias_tile(2 * g + 2 + j, j)
            load_v(DIFFO_U - 2, GROUPS - 1)
            closing(2)
            gate_up(1)
            closing(3)
            for t in range(ST - 1):
                sp.wait_ge(x_added, 3 * ST + t + 1)
                sp.dma_start(out[0, t * P:(t + 1) * P, :], x[:, t, :]).then_inc(out_done, 16)
            for half in range(2):
                cols = slice(half * D // 2, (half + 1) * D // 2)
                sp.wait_ge(x_added, 4 * ST + half)
                sp.dma_start(out[0, S - P:S, cols], x[:, ST - 1, cols]).then_inc(out_done, 16)
            sp.wait_ge(out_done, 16 * (ST + 1))

        @block.gpsimd
        def _(pool):
            nc.gpsimd.memset(expo[:], -0.5).then_inc(set_up, 1)
            nc.gpsimd.memset(eps[:], EPS).then_inc(set_up, 1)
            pool.wait_ge(set_up, 3)

            def rsqrt(mean_sq, ms_sem, ms_n, out_ap, done, cols):
                nc.gpsimd.tensor_tensor(out_ap, mean_sq, eps[:, 0:cols], ALU.add).then_inc(ms_sem, 1)
                pool.wait_ge(ms_sem, ms_n)
                nc.gpsimd.tensor_tensor(out_ap, out_ap, expo[:, 0:cols], ALU.pow).then_inc(done, 1)

            def pre(c, t):
                pool.wait_ge(pre_ssq, ST * c + t + 1)
                rsqrt(ssq[:, 4 + t:5 + t], pre_ms, ST * c + t + 1, rstd[:, 4 + t:5 + t], pre_rstd, 1)

            def post(c, t):
                pool.wait_ge(post_ssq, ST * c + t + 1)
                rsqrt(ssq[:, t:t + 1], post_ms, ST * c + t + 1, rstd[:, t:t + 1], post_rstd, 1)

            def boundary(c):
                post(c, 0)
                post(c, 1)
                if c == 3:
                    post(c, 2)
                    post(c, 3)
                    return
                pre(c + 1, 0)
                pre(c + 1, 1)
                post(c, 2)
                u = CLOSERS[c][0] + CLOSERS[c][1] + 1
                high, low = weight_parts(last_slots(c)[3])
                pool.wait_ge(w_hi_made, u + 1)
                nc.gpsimd.tensor_tensor(low[:, 0:HALF], raw[u % 2][:, 0:HALF], high[:, 0:HALF].bitcast(F32),
                                        ALU.subtract).then_inc(w_pool, 1)
                pre(c + 1, 2)
                post(c, 3)
                pre(c + 1, 3)

            for t in range(ST):
                pre(0, t)
            with pool.Fori(0, RET_HEADS) as h:
                pool.wait_ge(ret_ssq, ST * h + ST)
                rsqrt(ssq[:, 8:12], ret_ms, h + 1, rstd[:, 8:12], ret_rstd, ST)
            boundary(0)
            boundary(1)

            def scale_second(head, j):
                pool.wait_ge(lam_scaled, head + 1)
                for t in range(ST):
                    e1 = lg[j][:, 1, OFF[t]:OFF[t] + (t + 1) * P]
                    nc.gpsimd.tensor_tensor(e1, e1, stat[j][:, 20 + t:21 + t].to_broadcast([P, (t + 1) * P]),
                                            ALU.mult).then_inc(e1_scaled, 1)

            def o_norm(head, j):
                pool.wait_ge(o_ssq, head + 1)
                rsqrt(stat[j][:, 24:28], o_ms, head + 1, stat[j][:, 28:32], o_rstd, ST)

            with pool.Fori(0, GROUPS) as g:
                for j in range(GROUP):
                    scale_second(2 * g + j, j)
                for j in range(GROUP):
                    o_norm(2 * g + j, j)
            boundary(2)
            boundary(3)

        @block.scalar
        def _(act):
            act.dma_start(rel[0:BUCKETS, :], A["rel_bias_table"]).then_inc(rel_in, 16)
            act.dma_start(tmp[0:BUCKETS + 1, 0, 0:640], A["buckets"]).then_inc(rel_in, 16)
            lam_tile = tmp[:, 1, 640:640 + 4 * DIFF_DH]
            act.wait_ge(set_up, 3)
            nc.scalar.activation(lam[:, 6:7], expo[:, 0:1], ACT.Square).then_inc(warm, 1)

            def prep(u, slot, high=None, used=None, size=UNIT):
                act.wait_ge(w_used, (u - 1 if used is None else used) + PRIME)
                act.wait_ge(raw_in[slot], 8 * (u - slot) + 16)
                high = w_hi[slot][:] if high is None else high
                nc.scalar.activation(high, raw[slot][:, 0:size], ACT.Copy).then_inc(w_hi_made, 1)

            def mean_square(src, col, done, before):
                for s, count in before:
                    if isinstance(count, int) and count == 0:
                        continue
                    act.wait_ge(s, count)
                n = src.shape[-1]
                nc.scalar.activation(junk[:, 0:n], src, ACT.Square, scale=n ** -0.5, accum_out=ssq[:, col:col + 1]).then_inc(done, 1)

            def pre_square(c, t):
                if c == 0:
                    act.wait_ge(x_in[t], 16)
                else:
                    act.wait_ge(x_added, ST * (c - 1) + t + 1)
                before = [(pre_ssq, ST * c + t)]
                if c:
                    before.append((post_ssq, ST * (c - 1) + (2, 2, 3, 4)[t]))
                mean_square(x[:, t, :], 4 + t, pre_ssq, before)

            def pre_high(c, t):
                act.wait_ge(pre_turned, ST * c + t + 1)
                nc.scalar.activation(h_hi[:, :, t * P:(t + 1) * P],
                                     turned_rows(c, t), ACT.Copy).then_inc(h_hi_made, 1)

            def post_square(c, t):
                if t < ST - 1:
                    act.wait_ge(row_done, (ST - 1) * c + t + 1)
                else:
                    act.wait_ge(w_used, CLOSERS[c][0] + CLOSERS[c][1] + PRIME)
                before = [(post_ssq, ST * c + t)]
                if c < 3:
                    before.append((pre_ssq, ST * (c + 1) + (0, 0, 2, 3)[t]))
                mean_square(bank(2 * t, 2), t, post_ssq, before)

            def boundary(c):
                nxt = CLOSERS[c][0] + CLOSERS[c][1]
                if c == 3:
                    for t in range(ST):
                        post_square(c, t)
                    return
                slots = last_slots(c)
                post_square(c, 0)
                post_square(c, 1)
                pre_square(c + 1, 0)
                pre_square(c + 1, 1)
                prep(nxt, nxt % 2, weight_parts(slots[2])[0], used=nxt - 2)
                pre_high(c + 1, 0)
                post_square(c, 2)
                pre_high(c + 1, 1)
                prep(nxt + 1, (nxt + 1) % 2, weight_parts(slots[3])[0], used=nxt - 1)
                pre_square(c + 1, 2)
                post_square(c, 3)
                pre_square(c + 1, 3)
                pre_high(c + 1, 2)
                pre_high(c + 1, 3)

            def a_high(c, i, slot):
                src = (yT, hidden, oT, hidden)[c]
                nc.scalar.activation(act_parts[slot][0][:], src[:, bass.ds(2 * i, 2), :], ACT.Copy).then_inc(a_hi_made, 1)

            def closing(c):
                u0, n = CLOSERS[c]

                def step(i, par):
                    prep(u0 + i + 1, (u0 + par + 1) % 2)
                    a_high(c, i + 1, (u0 + par + 1) % 2)

                closing_steps(c, step, act)
                slots = last_slots(c)
                a_high(c, n - 2, 2)
                prep(u0 + n - 2, (u0 + n) % 2, weight_parts(slots[0])[0], used=u0 + n - 4 if slots[0] == 2 else None)
                prep(u0 + n - 1, (u0 + n - 1) % 2, weight_parts(slots[1])[0], used=u0 + n - 3)
                a_high(c, n - 1, (u0 + n) % 2)
                boundary(c)

            def gate_up(l):
                def step(i, first=False, last=False):
                    u = GU_U[l] + 2 * i
                    if first:
                        prep(u + 2, u % 2, used=u)
                    else:
                        prep(u + 1, (GU_U[l] + 1) % 2)
                    act.wait_ge(w_used, u + 1 + PRIME)
                    act.wait_ge(hid_made, 1 + FFN_N * l + i)
                    nc.scalar.activation(sil[:], bank(0, 2).rearrange("p (a s) -> p a s", a=2), ACT.Silu)\
                        .then_inc(sil_made, 1)
                    if not first:
                        prep(u + 2, GU_U[l] % 2)
                    if last:
                        a_high(2 * l + 1, 0, (u + 2) % 2)

                step(0, first=True)
                with act.Fori(1, FFN_N - 1) as i:
                    step(i)
                step(FFN_N - 1, last=True)

            pre_square(0, 0)
            pre_square(0, 1)
            act.wait_ge(first_in, 16)
            nc.scalar.activation(w_hi[0][:, 0:HALF], raw[0][:, 0:HALF], ACT.Copy).then_inc(first_hi_made, 1)
            pre_high(0, 0)
            act.wait_ge(raw_in[0], 16)
            nc.scalar.activation(w_hi[0][:, HALF:UNIT], raw[0][:, HALF:UNIT], ACT.Copy).then_inc(w_hi_made, 1)
            pre_square(0, 2)
            pre_high(0, 1)
            pre_square(0, 3)
            act.dma_start(lam_tile, spread(A["diff_lambda"][0][0], 4 * DIFF_DH)).then_inc(lam_in, 16)
            act.dma_start(subg[:, 0:1], A["diff_subln"].rearrange("a (d b) -> (a d) b", b=1)).then_inc(lam_in, 16)
            act.dma_start(cs[:], A["cos_sin"]).then_inc(cs_in, 16)
            act.dma_start(decay[:], A["decay"][:, 0:PACKED]).then_inc(decay_in, 16)
            pre_high(0, 2)
            pre_high(0, 3)
            act.wait_ge(bias_cp, 1)
            act.dma_start(bias_rows, tmp[0:DIFF_HEADS, 1, 0:640]).then_inc(bias_stored, 16)
            prep(1, 1, used=0)
            act.wait_ge(lam_sum, 2)
            nc.scalar.activation(lam[:, 2:4], lam[:, 0:2], ACT.Exp).then_inc(lam_exp, 1)

            def ret_head(h, last=False):
                u = 1 + RET_N * h
                for j in range(2):
                    prep(u + 1 + j, j)
                    act.wait_ge(rot_made, 2 * h + 1 + j)
                    nc.scalar.activation(qk_hi[:, 2 * j:2 * j + 2, :], tmp[:, 0, :].rearrange("p (a s) -> p a s", a=2),
                                         ACT.Copy).then_inc(qk_hi_made, 1)
                prep(u + 3, 0)
                for t in range(ST):
                    if t < ST - 1:
                        act.wait_ge(rv_row, (ST - 1) * h + t + 1)
                    else:
                        act.wait_ge(w_used, u + 3 + PRIME)
                    nc.scalar.activation(rv_hi[:, t, :], bank(4 + t), ACT.Copy).then_inc(rv_hi_made, 1)
                prep(u + 4, 1)
                act.wait_ge(inner_made, h + 1)
                nc.scalar.activation(in_hi[:], tmp[:].rearrange("p a d -> p (a d)")[:, 0:PACKED],
                                     ACT.Copy).then_inc(inner_hi_made, 1)
                prep(u + 5, 0)
                for t in range(ST):
                    act.wait_ge(ret_mm, ST * h + t + 1)
                    mean_square(bank(t), 8 + t, ret_ssq, [(ret_ssq, ST * h + t)] if t else [])
                if last:
                    a_high(0, 0, RETO_U % 2)
                for t in range(ST):
                    if t < ST - 1:
                        act.wait_ge(gate_row, (ST - 1) * h + t + 1)
                    else:
                        act.wait_ge(w_used, u + 5 + PRIME)
                    nc.scalar.activation(gated[:, t, :], bank(4 + t), ACT.Silu).then_inc(gate_made, 1)
                if not last:
                    prep(u + 6, 1)
                for t in range(ST):
                    act.wait_ge(y_turned, ST * h + t + 1)
                    nc.scalar.activation(yT[:, bass.ds(4 * h, 4), t * P:(t + 1) * P],
                                         bank(t).rearrange("p (a s) -> p a s", a=4), ACT.Copy).then_inc(yT_made, 1)

            with act.Fori(0, RET_HEADS - 1) as h:
                ret_head(h)
            act.wait_ge(bias_stored, 16)
            diagonals = bass.AP(tensor=bias_rows.tensor, offset=bias_rows.offset + P - 1, ap=[[640, DIFF_HEADS], [-1, P], [1, S]])
            act.dma_start(bias_tiles, diagonals).then_inc(bias_spread, 16)
            ret_head(RET_HEADS - 1, last=True)
            closing(0)
            gate_up(0)
            closing(1)

            def q_high(j, b):
                nc.scalar.activation(q_hi[:, j, :], bank(b), ACT.Copy, scale=-(DIFF_DH ** -0.5)).then_inc(q_hi_made, 1)

            def k_high(j, b):
                nc.scalar.activation(k_hi[:, j, :], bank(b), ACT.Copy).then_inc(k_hi_made, 1)

            def v_high(half, last=False):
                nc.scalar.activation(v_parts[:, 2 * half:2 * half + 2, :, 0, :], two_rows(half, last), ACT.Copy).then_inc(v_hi_made, 1)

            def exps(head, j):
                for n, (t, i) in enumerate(ORDER):
                    act.wait_ge(lg_made, 8 * head + n + 1)
                    e = lg[j][:, i, OFF[t]:OFF[t] + (t + 1) * P]
                    nc.scalar.activation(e, e, ACT.Exp, bias=stat[j][:, 4 * i + t:4 * i + t + 1], scale=-1.0,
                                         accum_out=stat[j][:, 8 + 4 * i + t:9 + 4 * i + t]).then_inc(exp_made, 1)

            def aT_high(head):
                act.wait_ge(a_turned, head + 1)
                nc.scalar.activation(aT_hi[:], turned_maps, ACT.Copy).then_inc(aT_hi_made, 1)

            def o_square(head, j):
                act.wait_ge(o_summed, head + 1)
                nc.scalar.activation(o_part(j, 0), o_n[j][:], ACT.Square, scale=DIFF_DV ** -0.5).then_inc(o_sq, 1)

            def oT_copy(head, j, b):
                act.wait_ge(o_turned, head + 1)
                nc.scalar.activation(oT[:, bass.ds(head, 1), :].rearrange("p a s -> p (a s)"), bank(b), ACT.Copy,
                                     scale=subg[:, 1:2]).then_inc(oT_made, 1)

            s0, s1 = DIFF_U % 2, (DIFF_U + 1) % 2

            def prep_v(u, used):
                prep(u, s0, spare_hi[:, 0:HALF], used, HALF)
                prep(u + 1, s1, spare_hi[:, HALF:UNIT], used, HALF)

            act.wait_ge(w_used, DIFF_U + 1 + PRIME)
            for j in range(GROUP):
                q_high(j, j)
            prep_v(DIFF_U + 2, DIFF_U + 1)
            act.wait_ge(k_tile, 1)
            k_high(0, 2)
            act.wait_ge(w_used, DIFF_U + 2 + PRIME)
            k_high(1, 3)

            with act.Fori(0, GROUPS - 1) as g:
                u = DIFF_U + 2 + DIFF_N * g
                head = 2 * g
                prep(u + 2, s0, used=u)
                exps(head, 0)
                prep(u + 3, s1, used=u)
                act.wait_ge(v_half, g + 1)
                v_high(0)
                act.wait_ge(w_used, u + 2 + PRIME)
                v_high(1)
                exps(head + 1, 1)
                act.wait_ge(q_tile, g + 1)
                q_high(0, q_bank[0])
                aT_high(head)
                act.wait_ge(w_used, u + 3 + PRIME)
                q_high(1, q_bank[1])
                aT_high(head + 1)
                o_square(head, 0)
                prep_v(u + 4, u + 2)
                act.wait_ge(k_tile, g + 2)
                k_high(0, k_bank[0])
                o_square(head + 1, 1)
                act.wait_ge(w_used, u + 4 + PRIME)
                k_high(1, k_bank[1])
                for j in range(GROUP):
                    oT_copy(head + j, j, oT_bank[j])
            g, head, u = GROUPS - 1, DIFF_HEADS - GROUP, DIFFO_U - 2
            prep(DIFFO_U, s0, used=u)
            exps(head, 0)
            act.wait_ge(v_half, g + 1)
            v_high(0)
            prep(DIFFO_U + 1, s1, used=u)
            act.wait_ge(qk_mm, head + 2)
            a_high(2, 0, 3)
            exps(head + 1, 1)
            act.wait_ge(w_used, u + 2 + PRIME)
            v_high(1, last=True)
            aT_high(head)
            a_high(2, 1, 4)
            prep(DIFFO_U + 2, s0, spare_hi[:], used=DIFFO_U)
            o_square(head, 0)
            aT_high(head + 1)
            oT_copy(head, 0, last_oT_bank[0])
            o_square(head + 1, 1)
            a_high(2, 2, 2)
            oT_copy(head + 1, 1, last_oT_bank[1])
            prep(DIFFO_U + 3, s1, w_hi[s0][:], used=DIFFO_U + 1)
            a_high(2, 3, 0)
            boundary(2)
            gate_up(1)
            closing(3)

        @block.vector
        def _(dve):
            nc.vector.memset(rel[BUCKETS:BUCKETS + 1, :], MASKED).then_inc(set_up, 1)
            dve.sem_inc(w_split, PRIME)
            dve.sem_inc(w_used, PRIME)
            dve.sem_inc(hid_made, 1)
            dve.sem_inc(yT_made, ST)
            dve.sem_inc(oT_made, 1)

            def low(out_ap, whole, high, done):
                nc.vector.tensor_tensor(out_ap, whole, high.bitcast(F32), ALU.subtract).then_inc(done, 1)

            def prep(u, slot, place=None):
                high, rest = weight_parts(slot if place is None else place)
                dve.wait_ge(w_hi_made, u + 1)
                low(rest, raw[slot][:], high, w_split)

            def pre_scale(c, t):
                dve.wait_ge(pre_rstd, ST * c + t + 1)
                if t == 0:
                    dve.wait_ge(gpre_in, 16 * (c + 1))
                if c == 0 and t >= 1:
                    dve.wait_ge(pre_turned, t)
                if c and t == 1:
                    dve.wait_ge(x_added, ST * (c - 1) + 1)
                if c and t == 2:
                    dve.wait_ge(pre_turned, ST * c + 1)
                nc.vector.scalar_tensor_tensor(out=tmp[:, pre_place(c, t), :], in0=x[:, t, :], scalar=rstd[:, 4 + t:5 + t],
                                               in1=g_pre[:], op0=ALU.mult, op1=ALU.mult).then_inc(pre_scaled, 1)

            def pre_low(c, t):
                dve.wait_ge(h_hi_made, ST * c + t + 1)
                low(h_lo[:, :, t * P:(t + 1) * P], turned_rows(c, t),
                    h_hi[:, :, t * P:(t + 1) * P], h_split)

            def post_scale(c, t):
                dve.wait_ge(post_rstd, ST * c + t + 1)
                if t == 0:
                    dve.wait_ge(gpost_in, 16 * (c + 1))
                if t >= 2:
                    dve.wait_ge(x_added, ST * c + t)
                if t == 3 and c < 3:
                    dve.wait_ge(pre_turned, ST * (c + 1) + 2)
                nc.vector.scalar_tensor_tensor(out=tmp[:, POST_PLACE[t], :], in0=bank(2 * t, 2),
                                               scalar=rstd[:, t:t + 1], in1=g_post[:],
                                               op0=ALU.mult, op1=ALU.mult).then_inc(post_scaled, 1)

            def post_add(c, t):
                dve.wait_ge(post_scaled, ST * c + t + 1)
                dve.wait_ge(x_added, ST * c + t)
                if (c, t) == (3, ST - 1):
                    for cols in (slice(0, D // 2), slice(D // 2, D)):
                        nc.vector.tensor_tensor(x[:, t, cols], x[:, t, cols], tmp[:, POST_PLACE[t], cols], ALU.add)\
                            .then_inc(x_added, 1)
                    return
                nc.vector.tensor_tensor(x[:, t, :], x[:, t, :], tmp[:, POST_PLACE[t], :], ALU.add).then_inc(x_added, 1)

            def boundary(c):
                for t in range(2 if c < 3 else ST):
                    post_scale(c, t)
                    post_add(c, t)
                if c == 3:
                    return
                nxt = CLOSERS[c][0] + CLOSERS[c][1]
                slots = last_slots(c)
                pre_scale(c + 1, 0)
                pre_scale(c + 1, 1)
                prep(nxt, nxt % 2, slots[2])
                pre_low(c + 1, 0)
                post_scale(c, 2)
                pre_low(c + 1, 1)
                post_add(c, 2)
                dve.wait_ge(w_hi_made, nxt + 2)
                dve.wait_ge(w_pool, c + 1)
                high, rest = weight_parts(slots[3])
                low(rest[:, HALF:UNIT], raw[(nxt + 1) % 2][:, HALF:UNIT], high[:, HALF:UNIT], w_split)
                post_scale(c, 3)
                post_add(c, 3)
                pre_scale(c + 1, 2)
                pre_scale(c + 1, 3)
                pre_low(c + 1, 2)
                pre_low(c + 1, 3)

            def a_low(c, i, slot):
                src = (yT, hidden, oT, hidden)[c]
                dve.wait_ge(a_hi_made, CLOSER_BASE[c] + i + 1)
                high, rest = act_parts[slot]
                low(rest[:], src[:, bass.ds(2 * i, 2), :], high[:], a_split)

            def closing(c):
                u0, n = CLOSERS[c]

                def step(i, par):
                    prep(u0 + i + 1, (u0 + par + 1) % 2)
                    a_low(c, i + 1, (u0 + par + 1) % 2)

                closing_steps(c, step, dve)
                slots = last_slots(c)
                a_low(c, n - 2, 2)
                prep(u0 + n - 2, (u0 + n) % 2, slots[0])
                prep(u0 + n - 1, (u0 + n - 1) % 2, slots[1])
                a_low(c, n - 1, (u0 + n) % 2)
                boundary(c)

            def gate_up(l):
                def step(i, first=False, last=False):
                    u = GU_U[l] + 2 * i
                    if not first:
                        prep(u + 1, (GU_U[l] + 1) % 2)
                    prep(u + 2, GU_U[l] % 2)
                    if last:
                        a_low(2 * l + 1, 0, (u + 2) % 2)
                    dve.wait_ge(sil_made, FFN_N * l + i + 1)
                    dve.wait_ge(w_used, u + 2 + PRIME)
                    nc.vector.tensor_tensor(hidden[:, bass.ds(2 * i, 2), :], sil[:],
                                            bank(2, 2).rearrange("p (a s) -> p a s", a=2), ALU.mult)\
                        .then_inc(hid_made, 1)

                step(0, first=True)
                with dve.Fori(1, FFN_N - 1) as i:
                    step(i)
                step(FFN_N - 1, last=True)

            pre_scale(0, 0)
            pre_scale(0, 1)
            dve.wait_ge(first_hi_made, 1)
            low(w_lo[0][:, 0:HALF], raw[0][:, 0:HALF], w_hi[0][:, 0:HALF], first_split)
            pre_low(0, 0)
            dve.wait_ge(w_hi_made, 1)
            low(w_lo[0][:, HALF:UNIT], raw[0][:, HALF:UNIT], w_hi[0][:, HALF:UNIT], w_split)
            pre_scale(0, 2)
            pre_low(0, 1)
            pre_scale(0, 3)
            pre_low(0, 2)
            dve.wait_ge(bias_mm, 1)
            nc.vector.tensor_copy(tmp[0:DIFF_HEADS, 1, 0:640], ps[0:DIFF_HEADS, 6 * BANK:6 * BANK + 640]).then_inc(bias_cp, 1)
            pre_low(0, 3)
            prep(1, 1)
            dve.wait_ge(lam_in, 32)
            lt = tmp[:, 1, 640:640 + 4 * DIFF_DH]
            for i in range(2):
                a, b = lt[:, 128 * i:128 * i + 64], lt[:, 128 * i + 64:128 * i + 128]
                nc.vector.tensor_tensor_reduce(out=junk[:, 64 * i:64 * i + 64],
                                               in0=a, in1=b, scale=1.0, scalar=0.0,
                                               op0=ALU.mult, op1=ALU.add, accum_out=lam[:, i:i + 1]).then_inc(lam_sum, 1)
            dve.wait_ge(lam_exp, 1)
            nc.vector.tensor_tensor(lam[:, 4:5], lam[:, 3:4], lam[:, 2:3], ALU.subtract).then_inc(lam_made, 1)
            nc.vector.tensor_scalar(subg[:, 1:2], subg[:, 0:1], 1.0 - LAMBDA_INIT, None, ALU.mult).then_inc(lam_made, 1)
            dve.wait_ge(lam_made, 2)
            nc.vector.tensor_scalar(lam[:, 5:6], lam[:, 4:5], -LAMBDA_INIT, None, ALU.add).then_inc(lam_made, 1)
            dve.wait_ge(bias_stored, 16)
            dve.wait_ge(cs_in, 16)

            def ret_head(h, last=False):
                u = 1 + RET_N * h
                ac = tmp[:, 0, :].rearrange("p (a s) -> p a s", a=2)
                bd = tmp[:, 1, :].rearrange("p (a s) -> p a s", a=2)
                for j in range(2):
                    prep(u + 1 + j, j)
                    dve.wait_ge(w_used, u + 1 + j + PRIME)
                    if j:
                        dve.wait_ge(qk_split, 2 * h + 1)
                    x1, x2 = bank(2 * j), bank(2 * j + 1)
                    nc.vector.tensor_tensor(ac[:, 0, :], x1, cs[:, 0, :], ALU.mult)
                    nc.vector.tensor_tensor(bd[:, 0, :], x2, cs[:, 1, :], ALU.mult)
                    nc.vector.tensor_tensor(ac[:, 1, :], x1, cs[:, 1, :], ALU.mult)
                    nc.vector.tensor_tensor(bd[:, 1, :], x2, cs[:, 0, :], ALU.mult).then_inc(rot_mul, 1)
                    dve.wait_ge(rot_mul, 2 * h + 1 + j)
                    nc.vector.tensor_tensor(ac[:, 0, :], ac[:, 0, :], bd[:, 0, :], ALU.subtract)
                    nc.vector.tensor_tensor(ac[:, 1, :], ac[:, 1, :], bd[:, 1, :], ALU.add).then_inc(rot_made, 1)
                    dve.wait_ge(qk_hi_made, 2 * h + 1 + j)
                    low(qk_lo[:, 2 * j:2 * j + 2, :], ac, qk_hi[:, 2 * j:2 * j + 2, :], qk_split)
                prep(u + 3, 0)
                for t in range(ST):
                    dve.wait_ge(rv_hi_made, ST * h + t + 1)
                    low(rv_lo[:, t, :], bank(4 + t), rv_hi[:, t, :], rv_split)
                prep(u + 4, 1)
                dve.wait_ge(inner_mm, h + 1)
                dve.wait_ge(decay_in, 16 * h + 16)
                inner = tmp[:].rearrange("p a d -> p (a d)")[:, 0:PACKED]
                nc.vector.tensor_tensor(inner, ps[:, 0:PACKED], decay[:], ALU.mult).then_inc(inner_made, 1)
                dve.wait_ge(inner_hi_made, h + 1)
                low(in_lo[:], inner, in_hi[:], inner_split)
                prep(u + 5, 0)
                if last:
                    a_low(0, 0, RETO_U % 2)
                dve.wait_ge(ret_rstd, h + 1)
                for t in range(ST):
                    dve.wait_ge(gate_made, ST * h + t + 1)
                    nc.vector.scalar_tensor_tensor(out=gated[:, t, :], in0=bank(t), scalar=rstd[:, 8 + t:9 + t],
                                                   in1=gated[:, t, :], op0=ALU.mult, op1=ALU.mult).then_inc(y_made, 1)
                if not last:
                    prep(u + 6, 1)

            with dve.Fori(0, RET_HEADS - 1) as h:
                ret_head(h)
            ret_head(RET_HEADS - 1, last=True)
            closing(0)
            gate_up(0)
            closing(1)

            def q_low(head, j, b):
                dve.wait_ge(q_hi_made, head + 1)
                nc.vector.scalar_tensor_tensor(out=q_lo[:, j, :], in0=bank(b), scalar=-(DIFF_DH ** -0.5),
                                               in1=q_hi[:, j, :].bitcast(F32), op0=ALU.mult,
                                               op1=ALU.subtract).then_inc(q_split, 1)

            def k_low(head, j, b):
                dve.wait_ge(k_hi_made, head + 1)
                low(k_lo[:, j, :], bank(b), k_hi[:, j, :], k_split)

            def v_low(g, half, last=False):
                dve.wait_ge(v_hi_made, 2 * g + half + 1)
                at = slice(2 * half, 2 * half + 2)
                low(v_parts[:, at, :, 1, :], two_rows(half, last), v_parts[:, at, :, 0, :], v_split)

            def logits(head, j):
                dve.wait_ge(qk_mm, head + 1)
                dve.wait_ge(nbias_in[j], 8 * (head - j) + 16)
                nc.vector.memset(stat[j][:, 32:33], 0.0).then_inc(inputs_seen, 1)
                dve.wait_ge(lam_made, 3)
                for n, (t, i) in enumerate(ORDER):
                    w = (t + 1) * P
                    nc.vector.tensor_tensor_reduce(out=lg[j][:, i, OFF[t]:OFF[t] + w], in0=scores(t, i),
                                                   in1=nbias[j][:, S - w:S], scale=1.0, scalar=3e38,
                                                   op0=ALU.add, op1=ALU.min,
                                                   accum_out=stat[j][:, 4 * i + t:4 * i + t + 1]).then_inc(lg_made, 1)

            def over_sums(head, j):
                st = stat[j]
                dve.wait_ge(inputs_seen, head + 1)
                dve.wait_ge(exp_made, 8 * head + 8)
                nc.vector.reciprocal(st[:, 16:24], st[:, 8:16]).then_inc(recip_made, 1)
                dve.wait_ge(recip_made, head + 1)
                nc.vector.tensor_scalar(st[:, 20:24], st[:, 20:24], lam[:, 5:6], None, ALU.mult).then_inc(lam_scaled, 1)

            def attn(head, j):
                for t in range(ST):
                    dve.wait_ge(e1_scaled, ST * head + t + 1)
                    w = (t + 1) * P
                    e0, e1 = (lg[j][:, i, OFF[t]:OFF[t] + w] for i in range(2))
                    nc.vector.scalar_tensor_tensor(out=e0, in0=e0, scalar=stat[j][:, 16 + t:17 + t], in1=e1,
                                                   op0=ALU.mult, op1=ALU.add).then_inc(attn_made, 1)

            def aT_low(head):
                dve.wait_ge(aT_hi_made, head + 1)
                low(aT_lo[:], turned_maps, aT_hi[:], aT_split)

            def o_sum(head, j):
                dve.wait_ge(o_mm, head + 1)
                parts = bank(o_bank[j], 2).rearrange("p (t a d) -> p t d a", t=ST, a=2)
                nc.vector.tensor_reduce(o_n[j][:], parts, AX_X, ALU.add).then_inc(o_summed, 1)

            def o_norm(head, j):
                st = stat[j]
                dve.wait_ge(o_sq, head + 1)
                nc.vector.tensor_reduce(st[:, 24:28], o_part(j, 0), AX_X, ALU.add).then_inc(o_ssq, 1)
                dve.wait_ge(o_rstd, head + 1)
                nc.vector.tensor_tensor(o_n[j][:], o_n[j][:],
                                        st[:, 28:32].unsqueeze(2).to_broadcast([P, ST, P]), ALU.mult)\
                    .then_inc(o_normed, 1)

            s0, s1 = DIFF_U % 2, (DIFF_U + 1) % 2

            def prep_v(u):
                for j, at in enumerate((slice(0, HALF), slice(HALF, UNIT))):
                    dve.wait_ge(w_hi_made, u + j + 1)
                    low(spare_lo[:, at], raw[(s0, s1)[j]][:, 0:HALF], spare_hi[:, at], w_split)

            for j in range(GROUP):
                q_low(j, j, j)
            prep_v(DIFF_U + 2)
            for j in range(GROUP):
                k_low(j, j, 2 + j)
            with dve.Fori(0, GROUPS - 1) as g:
                u = DIFF_U + 2 + DIFF_N * g
                head = 2 * g
                logits(head, 0)
                prep(u + 2, s0)
                over_sums(head, 0)
                prep(u + 3, s1)
                v_low(g, 0)
                attn(head, 0)
                v_low(g, 1)
                logits(head + 1, 1)
                q_low(head + 2, 0, q_bank[0])
                over_sums(head + 1, 1)
                aT_low(head)
                attn(head + 1, 1)
                q_low(head + 3, 1, q_bank[1])
                o_sum(head, 0)
                aT_low(head + 1)
                o_norm(head, 0)
                prep_v(u + 4)
                o_sum(head + 1, 1)
                k_low(head + 2, 0, k_bank[0])
                o_norm(head + 1, 1)
                k_low(head + 3, 1, k_bank[1])
            g, head = GROUPS - 1, DIFF_HEADS - GROUP
            logits(head, 0)
            prep(DIFFO_U, s0)
            over_sums(head, 0)
            v_low(g, 0)
            attn(head, 0)
            logits(head + 1, 1)
            a_low(2, 0, 3)
            prep(DIFFO_U + 1, s1)
            over_sums(head + 1, 1)
            v_low(g, 1, last=True)
            aT_low(head)
            attn(head + 1, 1)
            a_low(2, 1, 4)
            o_sum(head, 0)
            aT_low(head + 1)
            o_norm(head, 0)
            prep(DIFFO_U + 2, s0, 2)
            o_sum(head + 1, 1)
            o_norm(head + 1, 1)
            a_low(2, 2, 2)
            prep(DIFFO_U + 3, s1, s0)
            a_low(2, 3, 0)
            boundary(2)
            gate_up(1)
            closing(3)

        @block.tensor
        def _(pe):
            def three(out_ap, a_hi, a_lo, b_hi, b_lo, start, stop):
                nc.tensor.matmul(out_ap, a_hi, b_hi, start=start, stop=False)
                nc.tensor.matmul(out_ap, a_hi, b_lo, start=False, stop=False)
                return nc.tensor.matmul(out_ap, a_lo, b_hi, start=False, stop=stop)

            def column_tile(w, m, out_bank, cols=slice(0, S)):
                wh, wl = (x.rearrange("p (k n) -> p k n", k=KT)[:, :, m * P:(m + 1) * P] for x in w)
                for k in range(KT):
                    mm = three(bank(out_bank)[:, cols], wh[:, k, :], wl[:, k, :], h_hi[:, k, cols], h_lo[:, k, cols],
                               k == 0, k == KT - 1)
                return mm

            def columns(u, slot, banks):
                pe.wait_ge(w_split, u + 1 + PRIME)
                for m in range(2):
                    mm = column_tile(weight_parts(slot), m, banks[m])
                mm.then_inc(w_used, 1)

            def row_tile(w, t, tiles, out_ap, n, first, between=None):
                wh, wl = (x.rearrange("p (k n) -> p k n", k=tiles) for x in w)
                at = slice(t * P, (t + 1) * P)
                for k in range(tiles):
                    kk = first + k
                    if between:
                        between(k)
                    mm = three(out_ap, h_hi[:, kk, at], h_lo[:, kk, at], wh[:, k, :], wl[:, k, :], kk == 0, kk == KT - 1)
                return mm

            def ret_rows(u, slot, half, before=None, row_sem=None):
                pe.wait_ge(w_split, u + 1 + PRIME)
                for t in range(ST):
                    if before:
                        before(t)
                    mm = row_tile(weight_parts(slot), t, 4, bank(4 + t), RET_DV, 4 * half)
                    if row_sem is not None and t < ST - 1:
                        mm.then_inc(row_sem, 1)
                mm.then_inc(w_used, 1)

            def turn_rows(c, t):
                pe.wait_ge(pre_scaled, ST * c + t + 1)
                if c == 0 and t >= 2:
                    pe.wait_ge(h_split, t - 1)
                rows = turned_rows(c, t)
                for k in range(KT):
                    mm = nc.tensor.transpose(rows[:, k, :], tmp[:, pre_place(c, t), k * P:(k + 1) * P], ident[:])
                mm.then_inc(pre_turned, 1)

            def bank_part(weights, acts, b, k, start, stop):
                at, cols = slice(b // 2 * P, (b // 2 + 1) * P), slice(b % 2 * BANK, (b % 2 + 1) * BANK)
                wh, wl = (w.rearrange("p (k n) -> p k n", k=2) for w in weights)
                return three(bank(b), acts[0][:, k, at], acts[1][:, k, at], wh[:, k, cols], wl[:, k, cols], start, stop)

            def row(slot, act_slot, t, start=False, stop=False):
                for k in range(2):
                    for half in range(2):
                        mm = bank_part(weight_parts(slot), act_parts[act_slot], 2 * t + half, k,
                                       start and k == 0, stop and k == 1)
                return mm

            def ready(c, i):
                pe.wait_ge(w_split, CLOSERS[c][0] + i + 1 + PRIME)
                pe.wait_ge(a_split, CLOSER_BASE[c] + i + 1)

            def closing(c, order, between):
                u0 = CLOSERS[c][0]

                def step(i, par):
                    ready(c, i)
                    first = isinstance(i, int) and i == 0
                    slot = (u0 + par) % 2
                    for m, t in enumerate(order if first else range(ST)):
                        if first:
                            between(m)
                        mm = row(slot, slot, t, first)
                    mm.then_inc(w_used, 1)

                closing_steps(c, step, pe)
                last_rows(c, LAST_ROWS)

            def last_rows(c, rows):
                u0, n = CLOSERS[c]
                slots = last_slots(c)
                places = ((slots[2], slots[2]), (slots[0], 2), (slots[1], (u0 + n) % 2 if c != 2 else 0))
                for m, t in rows:
                    if t == 0:
                        ready(c, n - 3 + m)
                    if c < 3 and (m, t) == (2, 2):
                        turn_rows(c + 1, 0)
                    if c < 3 and (m, t) == (1, 3):
                        turn_rows(c + 1, 1)
                    mm = row(*places[m], t, stop=m == 2)
                    if t == ST - 1:
                        mm.then_inc(w_used, 1)
                    elif m == 2:
                        mm.then_inc(row_done, 1)

            def after_closing(c):
                u = CLOSERS[c][0] + CLOSERS[c][1]
                for half in range(2):
                    cols = slice(half * 256, half * 256 + 256)
                    pe.wait_ge(h_split, ST * (c + 1) + 2 * half + 2)
                    for j in range(2):
                        pe.wait_ge(w_split, u + j + 1 + PRIME)
                        for m in range(2):
                            mm = column_tile(weight_parts(last_slots(c)[2 + j]), m, 2 * j + m, cols)
                            if half == 0 and (j, m) == (1, 0):
                                turn_rows(c + 1, 2)
                                turn_rows(c + 1, 3)
                            if c == 1 and half == 1 and (j, m) == (1, 0):
                                mm.then_inc(k_tile, 1)
                        if half:
                            mm.then_inc(w_used, 1)

            def gate_up(l):
                after_closing(2 * l)
                pe.wait_ge(sil_made, FFN_N * l + 1)
                with pe.Fori(1, FFN_N) as i:
                    u = GU_U[l] + 2 * i
                    columns(u, GU_U[l] % 2, (0, 1))
                    pe.wait_ge(hid_made, 1 + FFN_N * l + i)
                    columns(u + 1, (GU_U[l] + 1) % 2, (2, 3))
                    pe.wait_ge(sil_made, FFN_N * l + i + 1)

            pe.wait_ge(const_in, 16)
            turn_rows(0, 0)
            turn_rows(0, 1)
            pe.wait_ge(rel_in, 32)
            pe.wait_ge(set_up, 3)
            for at, n in ((0, BANK), (BANK, 640 - BANK)):
                mm = nc.tensor.matmul(ps[0:DIFF_HEADS, 6 * BANK + at:6 * BANK + at + n], rel[:],
                                      tmp[0:BUCKETS + 1, 0, at:at + n], start=True, stop=True)
            mm.then_inc(bias_mm, 1)

            def first_rows(t):
                pe.wait_ge(h_split, t + 1)
                if t == 2:
                    pe.wait_ge(bias_cp, 1)

            pe.wait_ge(first_split, 1)
            for t in range(ST):
                first_rows(t)
                mm = row_tile(weight_parts(0), t, 4, bank(4 + t), RET_DV, 0,
                              between=lambda k: pe.wait_ge(w_split, 1 + PRIME) if (t, k) == (0, 2) else None)
                if t < 2:
                    turn_rows(0, 2 + t)
            mm.then_inc(w_used, 1)

            def turn_y(h):
                for t in range(ST):
                    pe.wait_ge(y_made, ST * h + t + 1)
                    for a in range(4):
                        mm = nc.tensor.transpose(bank(t)[:, a * P:(a + 1) * P], gated[:, t, a * P:(a + 1) * P], ident[:])
                    mm.then_inc(y_turned, 1)

            def ret_head(h, last=False):
                u = 1 + RET_N * h
                pe.wait_ge(yT_made, ST * h + ST)
                columns(u, 1, (0, 1))
                columns(u + 1, 0, (2, 3))
                ret_rows(u + 2, 1, 1, row_sem=rv_row)
                pe.wait_ge(qk_split, 2 * h + 2)
                for m in (0, 1, 3, 2):
                    n = (ST - m) * P
                    at = RET_OFF[ST - 1 - m]
                    for d in range(2):
                        ks = slice(m * P, (m + 1) * P)
                        mm = three(ps[:, at:at + n], qk_hi[:, 2 + d, ks], qk_lo[:, 2 + d, ks],
                                   qk_hi[:, d, m * P:S], qk_lo[:, d, m * P:S], d == 0, d == 1)
                mm.then_inc(inner_mm, 1)
                ret_rows(u + 3, 0, 0, before=lambda t: pe.wait_ge(rv_split, ST * h + t + 1))
                pe.wait_ge(inner_split, h + 1)
                for t in range(ST):
                    for m in range(t + 1):
                        at = RET_OFF[ST - 1 - m] + (t - m) * P
                        mm = three(bank(t), in_hi[:, at:at + P], in_lo[:, at:at + P], rv_hi[:, m, :], rv_lo[:, m, :],
                                   m == 0, m == t)
                    mm.then_inc(ret_mm, 1)
                ret_rows(u + 4, 1, 1, row_sem=gate_row)
                if not last:
                    def before(t):
                        pe.wait_ge(gate_made, ST * h + t + 1)
                        if t == ST - 1:
                            turn_y(h)

                    ret_rows(u + 5, 0, 0, before=before)

            with pe.Fori(0, RET_HEADS - 1) as h:
                ret_head(h)
            h = RET_HEADS - 1
            ret_head(h, last=True)

            def between_ret(m):
                if m < 2:
                    pe.wait_ge(gate_made, ST * h + 2 * m + 2)
                if m == 1:
                    turn_y(h)
                if m >= 2:
                    pe.wait_ge(yT_made, ST * RET_HEADS + 2 * (m - 1))

            def between_ffn(l):
                def between(m):
                    if m == 2:
                        pe.wait_ge(hid_made, 1 + FFN_N * (l + 1))
                return between

            closing(0, (2, 3, 0, 1), between_ret)
            gate_up(0)
            closing(1, (2, 3, 0, 1), between_ffn(0))

            def attention_scores(head, j):
                pe.wait_ge(q_split, head + 1)
                pe.wait_ge(k_split, head + 1)
                for n, pair in enumerate(PAIRS):
                    if n == len(PAIRS) - 1:
                        pe.wait_ge(shared_bank, head + 1)
                    for part in range(3):
                        for t, i in pair:
                            d = slice(DIFF_DH * i, DIFF_DH * (i + 1))
                            q = (q_hi, q_hi, q_lo)[part][d, j, t * P:(t + 1) * P]
                            k = (k_hi, k_lo, k_hi)[part][d, j, 0:(t + 1) * P]
                            mm = nc.tensor.matmul(scores(t, i), q, k, start=part == 0, stop=part == 2)
                            if n == 0 and part == 2 and t == 1:
                                mm.then_inc(shared_bank, 1)
                mm.then_inc(qk_mm, 1)

            def turn_maps(head, j):
                for t in range(ST):
                    pe.wait_ge(attn_made, ST * head + t + 1)
                    for k in range(t + 1):
                        at = slice(OFF[t] + k * P, OFF[t] + (k + 1) * P)
                        mm = nc.tensor.transpose(turned_maps[:, at], lg[j][:, 0, at], ident[:])
                mm.then_inc(a_turned, 1)

            def attention_out(head, j):
                pe.wait_ge(aT_split, head + 1)
                for t in range(ST):
                    o = bank(o_bank[j], 2)[:, t * 2 * P:(t + 1) * 2 * P]
                    for k in range(t + 1):
                        at = slice(OFF[t] + k * P, OFF[t] + (k + 1) * P)
                        v = v_parts[:, k, j].rearrange("p a d -> p (a d)")
                        nc.tensor.matmul(o, aT_hi[:, at], v, start=k == 0, stop=False)
                        mm = nc.tensor.matmul(o, aT_lo[:, at], v, start=False, stop=k == t)
                mm.then_inc(o_mm, 1)

            def turn_o(head, j, b):
                pe.wait_ge(o_normed, head + 1)
                for t in range(ST):
                    mm = nc.tensor.transpose(bank(b)[:, t * P:(t + 1) * P], o_n[j][:, t, :], ident[:])
                mm.then_inc(o_turned, 1)

            def v_tiles(half, last=False):
                for t in (2 * half, 2 * half + 1):
                    mm = row_tile(weight_parts(2), t, KT, v_rows(t, last), 256, 0)
                return mm

            s0, s1 = DIFF_U % 2, (DIFF_U + 1) % 2
            after_closing(1)
            pe.wait_ge(k_split, GROUP)
            with pe.Fori(0, GROUPS - 1) as g:
                u = DIFF_U + 2 + DIFF_N * g
                head = 2 * g
                attention_scores(head, 0)
                pe.wait_ge(oT_made, head + 1)
                pe.wait_ge(w_split, u + 2 + PRIME)
                v_tiles(0).then_inc(v_half, 1)
                v_tiles(1).then_inc(w_used, 2)
                pe.wait_ge(lg_made, 8 * head + 8)
                attention_scores(head + 1, 1)
                pe.wait_ge(w_split, u + 3 + PRIME)
                column_tile(weight_parts(s0), 0, q_bank[0]).then_inc(q_tile, 1)
                pe.wait_ge(v_split, 2 * g + 2)
                pe.wait_ge(lg_made, 8 * head + 16)
                turn_maps(head, 0)
                column_tile(weight_parts(s0), 1, q_bank[1]).then_inc(w_used, 1)
                attention_out(head, 0)
                turn_maps(head + 1, 1)
                pe.wait_ge(w_split, u + 4 + PRIME)
                pe.wait_ge(q_split, head + 4)
                column_tile(weight_parts(s1), 0, k_bank[0]).then_inc(k_tile, 1)
                attention_out(head + 1, 1)
                column_tile(weight_parts(s1), 1, k_bank[1]).then_inc(w_used, 1)
                pe.wait_ge(o_normed, head + 2)
                for j in range(GROUP):
                    turn_o(head + j, j, oT_bank[j])
            g, head, u = GROUPS - 1, DIFF_HEADS - GROUP, DIFFO_U - 2
            attention_scores(head, 0)
            pe.wait_ge(oT_made, head + 1)
            pe.wait_ge(w_split, u + 2 + PRIME)
            v_tiles(0).then_inc(v_half, 1)
            pe.wait_ge(lg_made, 8 * head + 8)
            attention_scores(head + 1, 1)
            v_tiles(1, last=True).then_inc(w_used, 2)

            def ahead(i, banks):
                ready(2, i)
                for b in banks:
                    for k in range(2):
                        mm = bank_part(weight_parts((s0, s1)[i]), act_parts[3 + i], b, k, (i, k) == (0, 0), False)
                return mm

            pe.wait_ge(lg_made, 8 * head + 16)
            pe.wait_ge(v_split, 2 * g + 1)
            turn_maps(head, 0)
            ahead(0, (0, 3))
            pe.wait_ge(v_split, 2 * g + 2)
            ahead(0, (7,))
            attention_out(head, 0)
            turn_maps(head + 1, 1)
            ahead(1, (0, 3, 7))
            attention_out(head + 1, 1)
            turn_o(head, 0, last_oT_bank[0])
            for i in range(2):
                ahead(i, (1, 2))
            turn_o(head + 1, 1, last_oT_bank[1])
            pe.wait_ge(oT_made, head + 2)
            ahead(0, (4, 5))
            pe.wait_ge(oT_made, head + 3)
            ahead(0, (6,)).then_inc(w_used, 1)
            last_rows(2, [(1, 0), (1, 1), (2, 0), (2, 1)])
            ahead(1, (4, 5, 6)).then_inc(w_used, 1)
            last_rows(2, [(1, 2), (2, 2), (1, 3), (2, 3)])
            gate_up(1)
            closing(3, (2, 3, 0, 1), between_ffn(1))


LAST_ROWS = [(0, 0), (0, 1), (1, 0), (1, 1), (2, 0), (2, 1), (0, 2), (1, 2), (0, 3), (2, 2), (1, 3), (2, 3)]
POST_PLACE = (0, 1, 1, 0)


def pre_place(c, t):
    return 2 if c == 0 else (2, 0, 2, 1)[t]


PAIRS = [[(1, 0), (0, 1)], [(3, 0), (3, 1)], [(2, 0), (2, 1)], [(0, 0), (1, 1)]]
ORDER = sum(PAIRS, [])


def constants():
    f32 = np.float32
    half = RET_DK // 2
    inv = f32(10000.0) ** (-np.arange(half, dtype=f32) / f32(half))
    ang = (np.arange(S, dtype=f32)[None, :] * inv[:, None]).astype(f32)
    cos_sin = np.stack([np.cos(ang), np.sin(ang)], 1).astype(f32)
    log_gamma = np.log1p(-(2.0 ** (-5.0 - np.arange(RET_HEADS))))
    decay = np.zeros((RET_HEADS, P, PACKED))
    key = np.arange(P)[:, None]
    for m in range(ST):
        n = (ST - m) * P
        d = np.arange(n)[None, :] - key
        at = RET_OFF[ST - 1 - m]
        decay[:, :, at:at + n] = np.where(d >= 0, np.exp(np.maximum(d, 0) * log_gamma[:, None, None]), 0.0)
    decay = (decay * RET_DK ** -0.5).astype(f32).transpose(1, 0, 2).reshape(P, RET_HEADS * PACKED)
    dist = np.arange(S)
    exact = BUCKETS // 2
    large = exact + (np.log(np.maximum(dist, 1).astype(f32) / f32(exact)) / f32(np.log(128 / exact))
                     * f32(BUCKETS - exact)).astype(np.int32)
    bucket = np.where(dist < exact, dist, np.minimum(large, BUCKETS - 1))
    buckets = np.zeros((BUCKETS + 1, 640), f32)
    buckets[bucket[::-1], np.arange(S)] = -1.0
    buckets[BUCKETS, S:] = 1.0
    return {"cos_sin": cos_sin, "decay": np.ascontiguousarray(decay), "buckets": buckets, "ident": np.eye(P, dtype=f32)}


NAMES = ["x", "norm_gains", "ret_w_in", "ret_w_out", "diff_w_in", "diff_w_out", "diff_lambda", "diff_subln",
         "rel_bias_table", "ffn_w_gate", "ffn_w_up", "ffn_w_down"]


def kernel(**inputs):
    import concourse.bacc as bacc
    from concourse.bass_utils import run_bass_kernel_spmd

    nc = bacc.Bacc("TRN2", target_bir_lowering=False, num_devices=1)
    arrays, args = {}, {}
    for name, a in [*((n, inputs[n]) for n in NAMES), *constants().items()]:
        a = np.ascontiguousarray(a)
        arrays[f"in_{name}"] = a
        args[name] = nc.dram_tensor(f"in_{name}", a.shape, mybir.dt.from_np(a.dtype), kind="ExternalInput").ap()
    out = nc.dram_tensor("out", (1, S, D), F32, kind="ExternalOutput").ap()
    build(nc, args, out)
    r = run_bass_kernel_spmd(nc, [arrays], core_ids=[0])
    return r.results[0]["out"]
```
